# Optimizing a Trainium2 kernel written in Bass

```python
import jax, jax.numpy as jnp
from jax import lax
import numpy as np

D_MODEL = 2048
BATCH = 1
SEQ = 256
DEPTH = 2

HEAD_DIM = 128
GDN_HEADS = 6
GDN_CHUNK = 64
CONV_K = 4
SG_GROUPS = 4
SG_CHUNK = 128
SA_HEADS = 6
IDX_HEADS = 16
IDX_DIM = 64
INDEX_TOPK = 256
Q_BLOCK = 128
MEM_LEN = 256
MEM_HEADS = 4
D_FF = 4 * D_MODEL
ROPE_THETA = 10000.0
NORM_EPS = 1e-6

D_A = GDN_HEADS * HEAD_DIM
D_B = SG_GROUPS * HEAD_DIM
D_C = SA_HEADS * HEAD_DIM
D_MIX = D_A + D_B + D_C
D_MEM = MEM_HEADS * HEAD_DIM
IN_WIDTHS = (3 * D_A, D_A, GDN_HEADS, GDN_HEADS, D_B, D_B, D_C, HEAD_DIM, HEAD_DIM,
             IDX_HEADS * IDX_DIM, IDX_DIM, IDX_HEADS)
D_IN = sum(IN_WIDTHS)
IN_SPLIT_POINTS = tuple(int(v) for v in np.cumsum(IN_WIDTHS)[:-1])

kernel_name = "hybrid_gdn_sgmlp_dsa_trunk"

def rms_norm(x, g):
    xf = x.astype(jnp.float32)
    y = xf * lax.rsqrt(jnp.mean(xf * xf, axis=-1, keepdims=True) + NORM_EPS)
    return (y * g.astype(jnp.float32)).astype(x.dtype)

def layer_norm(x, g, b):
    xf = x.astype(jnp.float32)
    mu = jnp.mean(xf, axis=-1, keepdims=True)
    var = jnp.mean(jnp.square(xf - mu), axis=-1, keepdims=True)
    y = (xf - mu) * lax.rsqrt(var + NORM_EPS) * g.astype(jnp.float32) + b.astype(jnp.float32)
    return y.astype(x.dtype)

def l2_normalize(x):
    xf = x.astype(jnp.float32)
    return xf * lax.rsqrt(jnp.sum(xf * xf, axis=-1, keepdims=True) + NORM_EPS)

def rope_tables(seq_len, dim):
    inv_freq = ROPE_THETA ** (-jnp.arange(0, dim, 2, dtype=jnp.float32) / dim)
    ang = jnp.arange(seq_len, dtype=jnp.float32)[:, None] * inv_freq[None, :]
    return jnp.cos(ang), jnp.sin(ang)

def apply_rope(x, cos, sin):
    half = x.shape[-1] // 2
    shape = (1, x.shape[1]) + (1,) * (x.ndim - 3) + (half,)
    c = cos.reshape(shape).astype(x.dtype)
    s = sin.reshape(shape).astype(x.dtype)
    x1, x2 = x[..., :half], x[..., half:]
    return jnp.concatenate([x1 * c - x2 * s, x2 * c + x1 * s], axis=-1)

def causal_depthwise_conv(x, w):
    c = x.shape[-1]
    return lax.conv_general_dilated(
        x, w.astype(x.dtype)[:, None, :], window_strides=(1,), padding=((CONV_K - 1, 0),),
        dimension_numbers=("NWC", "WIO", "NWC"), feature_group_count=c)

def gated_delta_rule_chunked(q, k, v, g, beta):
    b_, s_, h_, dk = q.shape
    dv = v.shape[-1]
    c_ = GDN_CHUNK
    n_ = s_ // c_

    def chunk(t):
        t = t.reshape((b_, n_, c_, h_) + t.shape[3:])
        return jnp.moveaxis(t, 3, 1)

    q = chunk(q) * (dk ** -0.5)
    k, v, g, beta = chunk(k), chunk(v), chunk(g), chunk(beta)
    g = jnp.cumsum(g, axis=-1)
    causal = jnp.tril(jnp.ones((c_, c_), dtype=bool))
    decay = jnp.exp(jnp.where(causal, g[..., :, None] - g[..., None, :], -jnp.inf))
    kb = k * beta[..., None]
    strict = jnp.tril(jnp.einsum('bhncd,bhnsd->bhncs', kb, k) * decay, -1)
    eye = jnp.eye(c_, dtype=jnp.float32)
    rhs = jnp.concatenate([v * beta[..., None], kb * jnp.exp(g)[..., None]], axis=-1)
    sol = lax.linalg.triangular_solve(strict + eye, rhs, left_side=True, lower=True,
                                      unit_diagonal=True)
    u, w = sol[..., :dv], sol[..., dv:]
    attn_intra = jnp.einsum('bhncd,bhnsd->bhncs', q, k) * decay
    q_dec = q * jnp.exp(g)[..., None]
    k_dec = k * jnp.exp(g[..., -1:] - g)[..., None]
    g_last = jnp.exp(g[..., -1])

    def step(state, xs):
        u_c, w_c, qd_c, kd_c, a_c, gl_c = xs
        v_new = u_c - jnp.matmul(w_c, state)
        o_c = jnp.matmul(qd_c, state) + jnp.matmul(a_c, v_new)
        state = state * gl_c[..., None, None] + jnp.matmul(jnp.swapaxes(kd_c, -1, -2), v_new)
        return state, o_c

    xs = tuple(jnp.moveaxis(t, 2, 0) for t in (u, w, q_dec, k_dec, attn_intra, g_last))
    state0 = jnp.zeros((b_, h_, dk, dv), jnp.float32)
    _, o = lax.scan(step, state0, xs)
    return jnp.transpose(o, (1, 0, 3, 2, 4)).reshape(b_, s_, h_, dv)

def spatial_gating(z_u, z_v, ln_g, ln_b, w_s, b_s):
    b_, s_, _ = z_v.shape
    v = layer_norm(z_v, ln_g, ln_b)
    v = v.reshape(b_, s_ // SG_CHUNK, SG_CHUNK, SG_GROUPS, HEAD_DIM)
    mask = jnp.tril(jnp.ones((SG_CHUNK, SG_CHUNK), dtype=bool))
    w = jnp.where(mask[None], w_s, 0.0).astype(v.dtype)
    s = jnp.einsum('gts,bcsgd->bctgd', w, v) + b_s.T.astype(v.dtype)[None, None, :, :, None]
    return z_u * s.reshape(b_, s_, D_B)

def indexer_sparse_attention(q, k, v, iq, ik, iw):
    b_, s_ = q.shape[:2]
    n_sel = min(INDEX_TOPK, s_ // 4)
    nb = s_ // Q_BLOCK
    key_pos = jnp.arange(s_)

    def blocks(t):
        return jnp.moveaxis(t.reshape((b_, nb, Q_BLOCK) + t.shape[2:]), 1, 0)

    def one_block(args):
        qb, iqb, iwb, tb = args
        rel = jax.nn.relu(jnp.einsum('bqhd,bsd->bqhs', iqb, ik).astype(jnp.float32))
        score = jnp.einsum('bqhs,bqh->bqs', rel, iwb.astype(jnp.float32))
        admissible = key_pos[None, :] <= tb[:, None]
        score = jnp.where(admissible[None], score, -jnp.inf)
        _, idx = lax.top_k(score, n_sel)
        k_sel = jax.vmap(lambda kk, ii: kk[ii])(k, idx)
        v_sel = jax.vmap(lambda vv, ii: vv[ii])(v, idx)
        logits = jnp.einsum('bqhd,bqkd->bqhk', qb, k_sel).astype(jnp.float32) * (HEAD_DIM ** -0.5)
        valid = idx <= tb[None, :, None]
        logits = jnp.where(valid[:, :, None, :], logits, -jnp.inf)
        p = jax.nn.softmax(logits, axis=-1).astype(v.dtype)
        return jnp.einsum('bqhk,bqkd->bqhd', p, v_sel)

    t_pos = jnp.arange(s_).reshape(nb, Q_BLOCK)
    out = lax.map(one_block, (blocks(q), blocks(iq), blocks(iw), t_pos))
    return jnp.moveaxis(out, 0, 1).reshape(b_, s_, SA_HEADS, HEAD_DIM)

def hybrid_mixer(xn, w_in, conv_w, a_log, dt_bias, gdn_norm, sg_ln_g, sg_ln_b, sg_w, sg_b, w_out,
                 cos_h, sin_h, cos_i, sin_i):
    b_, s_, _ = xn.shape
    h = xn @ w_in
    (a_qkv, a_z, a_dec, a_beta, b_u, b_v, c_q, c_k, c_v, i_q, i_k, i_w) = jnp.split(
        h, IN_SPLIT_POINTS, axis=-1)

    qkv = jax.nn.silu(causal_depthwise_conv(a_qkv, conv_w))
    gq, gk, gv = jnp.split(qkv, 3, axis=-1)
    gq = l2_normalize(gq.reshape(b_, s_, GDN_HEADS, HEAD_DIM))
    gk = l2_normalize(gk.reshape(b_, s_, GDN_HEADS, HEAD_DIM))
    gv = gv.reshape(b_, s_, GDN_HEADS, HEAD_DIM).astype(jnp.float32)
    beta = jax.nn.sigmoid(a_beta.astype(jnp.float32))
    g = -jnp.exp(a_log.astype(jnp.float32)) * jax.nn.softplus(
        a_dec.astype(jnp.float32) + dt_bias.astype(jnp.float32))
    o_a = gated_delta_rule_chunked(gq, gk, gv, g, beta)
    z = a_z.reshape(b_, s_, GDN_HEADS, HEAD_DIM).astype(jnp.float32)
    o_a = (rms_norm(o_a, gdn_norm) * jax.nn.silu(z)).astype(xn.dtype).reshape(b_, s_, D_A)

    o_b = spatial_gating(jax.nn.gelu(b_u), jax.nn.gelu(b_v), sg_ln_g, sg_ln_b, sg_w, sg_b)

    q = apply_rope(c_q.reshape(b_, s_, SA_HEADS, HEAD_DIM), cos_h, sin_h)
    k = apply_rope(c_k, cos_h, sin_h)
    iq = apply_rope(i_q.reshape(b_, s_, IDX_HEADS, IDX_DIM), cos_i, sin_i)
    ik = apply_rope(i_k, cos_i, sin_i)
    iw = i_w * ((IDX_HEADS ** -0.5) * (IDX_DIM ** -0.5))
    o_c = indexer_sparse_attention(q, k, c_v, iq, ik, iw).reshape(b_, s_, D_C)

    return jnp.concatenate([o_a, o_b, o_c], axis=-1) @ w_out

def memory_cross_attention(xn, mn, w_q, w_kv, w_o):
    b_, s_, _ = xn.shape
    m_ = mn.shape[1]
    q = (xn @ w_q).reshape(b_, s_, MEM_HEADS, HEAD_DIM)
    k, v = jnp.split(mn @ w_kv, 2, axis=-1)
    k = k.reshape(b_, m_, MEM_HEADS, HEAD_DIM)
    v = v.reshape(b_, m_, MEM_HEADS, HEAD_DIM)
    logits = jnp.einsum('bshd,bmhd->bhsm', q, k).astype(jnp.float32) * (HEAD_DIM ** -0.5)
    p = jax.nn.softmax(logits, axis=-1).astype(v.dtype)
    o = jnp.einsum('bhsm,bmhd->bshd', p, v).reshape(b_, s_, D_MEM)
    return o @ w_o

def setup_inputs(seed: int = 0) -> dict:
    key = jax.random.key(seed)
    ks = jax.random.split(key, 24)

    def nrm(k, shape, scale):
        return jax.random.normal(k, shape, jnp.float32) * scale

    def gain(k, shape):
        return 1.0 + 0.02 * jax.random.normal(k, shape, jnp.float32)

    dt = jnp.exp(jax.random.uniform(ks[5], (DEPTH, GDN_HEADS), jnp.float32,
                                    minval=float(np.log(1e-3)), maxval=float(np.log(1e-1))))
    return {
        "x": nrm(ks[0], (BATCH, SEQ, D_MODEL), 1.0),
        "mem": nrm(ks[1], (BATCH, MEM_LEN, D_MODEL), 1.0),
        "ln_mix": gain(ks[2], (DEPTH, D_MODEL)),
        "w_in": nrm(ks[3], (DEPTH, D_MODEL, D_IN), D_MODEL ** -0.5),
        "conv_w": nrm(ks[4], (DEPTH, CONV_K, 3 * D_A), CONV_K ** -0.5),
        "a_log": jnp.log(jax.random.uniform(ks[6], (DEPTH, GDN_HEADS), jnp.float32, minval=1.0, maxval=16.0)),
        "dt_bias": dt + jnp.log(-jnp.expm1(-dt)),
        "gdn_norm": gain(ks[7], (DEPTH, HEAD_DIM)),
        "sg_ln_g": gain(ks[8], (DEPTH, D_B)),
        "sg_ln_b": nrm(ks[9], (DEPTH, D_B), 0.02),
        "sg_w": nrm(ks[10], (DEPTH, SG_GROUPS, SG_CHUNK, SG_CHUNK), SG_CHUNK ** -0.5),
        "sg_b": gain(ks[11], (DEPTH, SG_GROUPS, SG_CHUNK)),
        "w_out": nrm(ks[12], (DEPTH, D_MIX, D_MODEL), D_MIX ** -0.5),
        "ln_cross": gain(ks[13], (DEPTH, D_MODEL)),
        "ln_mem": gain(ks[14], (DEPTH, D_MODEL)),
        "w_q_mem": nrm(ks[15], (DEPTH, D_MODEL, D_MEM), D_MODEL ** -0.5),
        "w_kv_mem": nrm(ks[16], (DEPTH, D_MODEL, 2 * D_MEM), D_MODEL ** -0.5),
        "w_o_mem": nrm(ks[17], (DEPTH, D_MEM, D_MODEL), D_MEM ** -0.5),
        "ln_mlp": gain(ks[18], (DEPTH, D_MODEL)),
        "w_up": nrm(ks[19], (DEPTH, D_MODEL, D_FF), D_MODEL ** -0.5),
        "w_down": nrm(ks[20], (DEPTH, D_FF, D_MODEL), D_FF ** -0.5),
        "ln_final": gain(ks[21], (D_MODEL,)),
    }

def reference(x, mem, ln_mix, w_in, conv_w, a_log, dt_bias, gdn_norm, sg_ln_g, sg_ln_b, sg_w, sg_b,
              w_out, ln_cross, ln_mem, w_q_mem, w_kv_mem, w_o_mem, ln_mlp, w_up, w_down, ln_final):
    s_ = x.shape[1]
    cos_h, sin_h = rope_tables(s_, HEAD_DIM)
    cos_i, sin_i = rope_tables(s_, IDX_DIM)
    for l in range(DEPTH):
        h = rms_norm(x, ln_mix[l])
        x = x + hybrid_mixer(h, w_in[l], conv_w[l], a_log[l], dt_bias[l], gdn_norm[l], sg_ln_g[l],
                             sg_ln_b[l], sg_w[l], sg_b[l], w_out[l], cos_h, sin_h, cos_i, sin_i)
        x = x + memory_cross_attention(rms_norm(x, ln_cross[l]), rms_norm(mem, ln_mem[l]),
                                       w_q_mem[l], w_kv_mem[l], w_o_mem[l])
        h = rms_norm(x, ln_mlp[l])
        x = x + jnp.square(jax.nn.relu(h @ w_up[l])) @ w_down[l]
    return rms_norm(x, ln_final)


_drawn_inputs = setup_inputs


def setup_inputs(seed=0):
    import zlib

    import numpy as np

    out = dict(_drawn_inputs(seed))
    spreads = {}
    factors = {'gdn_norm': 5.606,
     'sg_ln_g': 7.856,
     'sg_ln_b': 8.0,
     'sg_b': 6.166,
     'ln_cross': 8.0,
     'ln_mem': 8.0,
     'ln_final': 7.671,
     'ln_mlp': 2.899}
    for name, (base, spread) in spreads.items():
        noise = np.random.default_rng([zlib.crc32(name.encode()), seed]).standard_normal(out[name].shape)
        drawn = base * np.exp(spread * noise) if base else spread * noise
        out[name] = __import__('jax').numpy.asarray(drawn.astype(out[name].dtype))
    for name, factor in factors.items():
        out[name] = (out[name] * factor).astype(out[name].dtype)
    return out
```

```python
from contextlib import ExitStack

import numpy as np

import concourse.bass as bass
from concourse import mybir

F32 = mybir.dt.float32
F32R = mybir.dt.float32r
I32 = mybir.dt.int32
ALU = mybir.AluOpType
ACT = mybir.ActivationFunctionType
AX = mybir.AxisListType

P = 128
D_MODEL, SEQ, DEPTH, MEM_LEN = 2048, 256, 2, 256
NT = SEQ // P
KT = D_MODEL // P
HEAD = 128
GDN_HEADS, SG_GROUPS, SA_HEADS, IDX_HEADS, IDX_DIM, MEM_HEADS = 6, 4, 6, 16, 64, 4
CONV_K, TOPK, EPS = 4, SEQ // 4, 1e-6
D_A, D_B, D_C, D_MEM, D_FF = GDN_HEADS * HEAD, SG_GROUPS * HEAD, SA_HEADS * HEAD, MEM_HEADS * HEAD, 4 * D_MODEL
GH = GDN_HEADS // 2
NC = GH * NT
LEVELS = 7
COL = 512
RING = 4
NEG, TAKEN, OFF = -1e38, -3e38, 1e30
SCALE = HEAD ** -0.5

C_QKV, C_Z, C_DEC = 0, 3 * D_A, 4 * D_A
C_BU = C_DEC + 2 * GDN_HEADS
C_BV, C_Q = C_BU + D_B, C_BU + 2 * D_B
C_IQ = C_Q + D_C + 2 * HEAD
C_IK = C_IQ + IDX_HEADS * IDX_DIM
D_IN = C_IK + IDX_DIM + IDX_HEADS
ZREST = C_BU - (C_Z + COL)
IREST = D_IN - C_IK
IW = IDX_HEADS * IDX_DIM + IREST

CONST = {}
_at = 0
for _name, _w in (("ident", P), ("tri", P), ("strict", P), ("incl", P), ("ones", P), ("level", LEVELS * P),
                  ("cos_h", NT * 64), ("sin_h", NT * 64), ("cos_i", NT * 32), ("sin_i", NT * 32)):
    CONST[_name] = (_at, _at + _w)
    _at += _w
N_CONST = _at


def shape_constants():
    c = np.zeros((P, N_CONST), np.float32)
    p, f = np.arange(P)[:, None], np.arange(P)[None, :]

    def put(name, a):
        c[:, CONST[name][0]:CONST[name][1]] = a

    put("ident", p == f)
    put("tri", p <= f)
    put("strict", np.where(f < p, 0, OFF))
    put("incl", np.where(f >= p, 0, OFF))
    put("ones", 1)
    lev = [((p >> b) % 2 == 1) & ((f >> b) == (p >> b) - 1) for b in range(LEVELS)]
    put("level", np.concatenate(lev, 1))
    for name, dim in (("h", HEAD), ("i", IDX_DIM)):
        inv = np.float32(10000.0) ** (-np.arange(0, dim, 2, dtype=np.float32) / np.float32(dim))
        ang = np.arange(SEQ, dtype=np.float32)[:, None] * inv.astype(np.float32)[None, :]
        for fn, what in ((np.cos, "cos_"), (np.sin, "sin_")):
            put(what + name, fn(ang).astype(np.float32).reshape(NT, P, dim // 2).transpose(1, 0, 2).reshape(P, -1))
    return c


class Unit:

    def __init__(self, name, mat, r0, tiles, c0, width, form, act):
        self.name, self.mat, self.r0, self.tiles, self.c0 = name, mat, r0, tiles, c0
        self.width, self.form, self.act = width, form, act
        self.pieces = tiles // 2


def layer_units():
    u = []

    def add(name, mat, c0, width, form="tok", act="A", r0=0, tiles=KT):
        u.append(Unit(name, mat, r0, tiles, c0, width, form, act))

    add("B1", "w_in", C_BV, D_B)
    add("B0", "w_in", C_BU, D_B)
    add("I0", "w_in", C_IQ, COL)
    add("I1", "w_in", C_IQ + COL, COL)
    add("I2", "w_in", C_IK, IREST)
    add("C0", "w_in", C_Q, COL)
    add("C1", "w_in", C_Q + COL, COL)
    for g in range(2):
        if g == 1:
            add("Z1", "w_in", C_Z + COL, ZREST)
        for s in range(3):
            add(f"{'QKV'[s]}{g}", "w_in", C_QKV + s * D_A + g * GH * HEAD, GH * HEAD, "ch")
    add("Z0", "w_in", C_Z, COL)
    for j in range(4):
        add(f"O{j}", "w_out", j * COL, COL, act="B")
    add("KM", "w_kv_mem", 0, D_MEM, "ch")
    add("VM", "w_kv_mem", D_MEM, D_MEM)
    add("QM", "w_q_mem", 0, D_MEM, "ch")
    for j in range(4):
        add(f"OM{j}", "w_o_mem", j * COL, COL, act="B", tiles=MEM_HEADS)
    for q in range(4):
        for j in range(4):
            add(f"U{q}{j}", "w_up", q * D_MODEL + j * COL, COL)
        for j in range(4):
            add(f"D{q}{j}", "w_down", j * COL, COL, act="B", r0=q * D_MODEL)
    at = 0
    for n, x in enumerate(u):
        x.n, x.first = n, at
        at += x.pieces
    return u, at


def trunk(nc, consts, x, mem, ln_mix, w_in, conv_w, a_log, dt_bias, gdn_norm, sg_ln_g, sg_ln_b, sg_w, sg_b,
          w_out, ln_cross, ln_mem, w_q_mem, w_kv_mem, w_o_mem, ln_mlp, w_up, w_down, ln_final, out):
    units, PIECES = layer_units()
    U = {u.name: u for u in units}
    matrices = dict(w_in=w_in, w_out=w_out, w_q_mem=w_q_mem, w_kv_mem=w_kv_mem, w_o_mem=w_o_mem, w_up=w_up,
                    w_down=w_down)
    assert PIECES % RING == 0 and len(units) % 2 == 0

    with ExitStack() as ctx:
        def sb(name, shape, dt=F32):
            return ctx.enter_context(nc.sbuf_tensor(name, shape, dt))

        def sem(name):
            return ctx.enter_context(nc.semaphore(name))

        x_res = sb("x_res", [P, NT, D_MODEL])
        act = {a: (sb(f"act{a}_hi", [P, KT, SEQ], F32R), sb(f"act{a}_lo", [P, KT, SEQ], F32R)) for a in "AB"}
        w_raw = sb("w_raw", [P, RING, 2, COL])
        w_hi = sb("w_hi", [P, RING, 2, COL], F32R)
        w_lo = sb("w_lo", [P, RING, 2, COL], F32R)
        const = sb("const", [P, N_CONST])
        par_rows = sb("par_rows", [P, 2, P])
        par = sb("par", [P, 2, P])
        ln_rows = sb("ln_rows", [P, 2, D_B])
        sgw = sb("sgw", [P, SG_GROUPS, P])
        sgw_t = sb("sgw_t", [P, SG_GROUPS, P])
        small = sb("small", [P, 544])
        scratch = sb("scratch", [P, 15360])
        psum = ctx.enter_context(nc.psum_tensor("psum", [P, 8, COL], F32))

        def cst(name, n=None):
            a = const[:, CONST[name][0]:CONST[name][1]]
            return a.rearrange("p (t n) -> p t n", t=n) if n else a

        ident, ones = cst("ident"), cst("ones")
        level = cst("level", LEVELS)

        def region(start, *shape):
            n = int(np.prod(shape))
            a = scratch[:, start:start + n]
            if len(shape) == 2:
                a = a.rearrange("p (a b) -> p a b", b=shape[1])
            if len(shape) == 3:
                a = a.rearrange("p (a b c) -> p a b c", b=shape[1], c=shape[2])
            return a

        xs = region(0, NT, D_MODEL)
        q_t = [region(g * 768, GH, SEQ) for g in range(2)]
        k_t, v_t = region(1536, GH, SEQ), region(2304, GH, SEQ)
        x_pad = region(3072, GH, SEQ + CONV_K - 1)
        kn, kn_t, vb, dec, dec_t, amat, aoff, rmat, umat, tmat = [region(3856 + 768 * i, NC, P) for i in range(10)]
        s1, w1 = region(11536, GH, P), region(11920, GH, P)
        qs = region(12304, GH, P)
        zz = region(12688, NT, D_A)
        vn, obuf, ksc = aoff, amat, tmat
        trig, sqq, sqk = aoff, rmat, amat
        ibuf, cbuf = region(3856, NT, IW), region(6064, NT, 1024)
        tmp_a, tmp_b = region(8112, NT, 1104), region(10320, NT, 1104)
        iq_t, p_t = region(8112, NT, 8, P), region(8112, SA_HEADS, NT, P)
        cq_t, ck_t, ik_t = region(10320, SA_HEADS, SEQ), region(11856, SEQ), region(12112, SEQ)
        ik2 = region(12528, NT, P)
        rope_a, rope_b = region(0, NT, 896), region(1792, NT, 896)
        relu = region(12784, 2, COL)
        score, work, mbias = region(13808, NT, SEQ), region(14320, NT, SEQ), region(14832, NT, SEQ)
        logit = region(3856, SA_HEADS, SEQ)
        zu, zv, sq_junk = region(12784, NT, D_B), region(13808, NT, D_B), region(10320, NT, D_B)
        mem_x = region(4096, NT, D_MODEL)
        qm_t, km_t, vm = region(8192, MEM_HEADS, SEQ), region(9216, MEM_HEADS, MEM_LEN), region(10240, NT, D_MEM)
        xlogit, xp_t = region(11264, NT, MEM_HEADS, MEM_LEN), region(13312, MEM_HEADS, NT, SEQ)
        h_relu, h_sq = region(4096, 2, 1024), region(6144, 2, 1024)
        fin_row, fin = region(4096, D_MODEL), region(8192, NT, D_MODEL)

        _sm = [0]

        def tiny(n):
            _sm[0] += n
            assert _sm[0] <= 544
            return small[:, _sm[0] - n:_sm[0]]

        ssq, ssq_mem = tiny(8), tiny(2)
        y_in, y_a, y_b, y_r = tiny(16), tiny(16), tiny(16), tiny(16)
        r_norm, r_qk, r_o = tiny(2), tiny(12), tiny(NC)
        al, dtb = tiny(GDN_HEADS), tiny(GDN_HEADS)
        db = tiny(NT * 12)
        t_abs, t_ln, gate, beta, eal = tiny(12), tiny(12), tiny(12), tiny(12), tiny(6)
        gcum, ngcum, eg, beg = tiny(12), tiny(12), tiny(12), tiny(12)
        glast, egl = tiny(GH), tiny(GH)
        mean, rstd, mcol = tiny(2), tiny(2), tiny(4)
        iw = tiny(NT * IDX_HEADS)
        max8 = tiny(8 * 16)
        smax, ssum, sinv = tiny(12), tiny(12), tiny(12)
        xmax, xsum, xinv = tiny(8), tiny(8), tiny(8)
        o_c, o_f = tiny(NC), tiny(NC)
        act_junk = tiny(1)

        PAR_ROWS = (4 * KT + SG_GROUPS + 1, CONV_K * 3 * GDN_HEADS)
        PAR = dict(ln_mix=(0, 0), ln_cross=(0, 16), ln_mem=(0, 32), ln_mlp=(0, 48), sg_b=(0, 64), gdn=(0, 68))

        def gain(name, i):
            row, at = PAR[name]
            return par[:, row, at + i:at + i + 1]

        def conv_tap(j, ct):
            return par[:, 1, j * 18 + ct:j * 18 + ct + 1]

        w_landed = [sem(f"w_landed{i}") for i in range(RING)]
        hi_ready, lo_ready = sem("hi_ready"), sem("lo_ready")
        piece_done = sem("piece_done")
        pair_free = [sem(f"pair_free{i}") for i in range(2)]
        bank_full = [sem(f"bank_full{i}") for i in range(4)]
        bank_free = [sem(f"bank_free{i}") for i in range(4)]
        PER_LAYER = {}
        counts = {}
        sems = {}

        def declare(**kw):
            for name, n in kw.items():
                PER_LAYER[name] = n
                sems[name] = sem(name)
                counts[name] = 0

        BASE = dict(ssq_ready=8, x_landed=0, const_landed=0, final_done=0)

        def at(name, l, i):
            assert 0 < i <= PER_LAYER[name] or (i == 0), (name, i)
            return sems[name], BASE.get(name, 0) + l * PER_LAYER[name] + i

        def signal(ins, name):
            counts[name] += 1
            return ins.then_inc(sems[name], 1)

        declare(
            params_landed=9 * 16, rows_landed=3 * 16, mem_landed=2 * 16,
            ssq_ready=24,
            xs_ready=12,
            act_hi=64, gdn_hi=6, gate_hi=4, att_hi=4, xat_hi=4, ffn_hi=32,
            mem_ssq=2, mem_scaled=4,
            gate_nmean=1, gate_var=2, gate_norm=2, gate_v=2, gate_w=1,
            rope_b=4, rope_done=5, relu_used=12, score_done=2, masked=2, topk_done=2, mask_ready=1,
            logits_ready=2, att_exp=12, att_p=2,
            conv_out=6, silu_out=6, sqs=4,
            db_ready=1, abs_ready=1, beta_exp=1, dec_ln=1, eal_ready=1, gate_g=1, beta_ready=1,
            eg_ready=1, beg_ready=1, trig_ready=2, kd_arg=2, egl_ready=2, dec_val=4, off_ready=14, t_ready=2,
            ksc_ready=4, o_ready=2,
            xlog_ready=2, xexp=8, xp_ready=2,
            h_sq_ready=16,
        )
        fin_sem, out_sem, start_sem = sem("final_scaled"), sem("out_landed"), sem("start_landed")
        fin_row_sem, pad_zero = sem("fin_row_landed"), sem("pad_zero")

        class Chain:

            def __init__(self, eng, name, per_layer):
                self.eng, self.sem, self.per, self.k, self.base = eng, sem(name), per_layer, 0, 0

            def run(self, ins):
                self.k += 1
                ins.then_inc(self.sem, 1)

            def settle(self, l):
                self.eng.wait_ge(self.sem, self.base + l * self.per + self.k)

            def link(self, l, ins):
                self.run(ins)
                self.settle(l)

            def end_layer(self):
                assert self.k == self.per, (self.sem, self.k)
                self.k = 0

        def wait(eng, s, v):
            if not (isinstance(v, int) and v <= 0):
                eng.wait_ge(s, v)

        uses, piece_before = {}, {}
        USES = 272
        BPL = USES // 4

        def bank_of(name):
            n = uses[name]
            return psum[:, 4 + n % 4, :]

        def wait_full(eng, l, name):
            n = uses[name]
            eng.wait_ge(bank_full[n % 4], l * BPL + n // 4 + 1)

        def free(ins, name):
            ins.then_inc(bank_free[uses[name] % 4], 1)

        def wait_freed(eng, l, name):
            n = uses[name]
            eng.wait_ge(bank_free[n % 4], l * BPL + n // 4 + 1)

        def score_head(n, i, per):
            return 2 * (n // 2 * per + i) + n % 2

        def pair(u):
            i = 2 * (u.n % 2)
            return psum[:, i:i + 2, :]

        def pair_ch(u):
            return pair(u).rearrange("p a (c t) -> p (a c) t", t=SEQ)

        def wait_unit(eng, l, u):
            eng.wait_ge(piece_done, l * PIECES + u.first + u.pieces)

        def free_pair(ins, u):
            ins.then_inc(pair_free[u.n % 2], 1)

        def wait_pair_freed(eng, l, u):
            eng.wait_ge(pair_free[u.n % 2], l * (len(units) // 2) + u.n // 2 + 1)

        block = ctx.enter_context(nc.Block())

        @block.tensor
        def _(pe):
            tp = nc.tensor.transpose

            def mm(o, a, b, start=True, stop=True, **kw):
                return nc.tensor.matmul(o, a, b, start=start, stop=stop, **kw)

            cnt, last_piece = [0], [-1]

            def take(l, name):
                n = cnt[0]
                cnt[0] += 1
                uses[name] = n
                piece_before[name] = last_piece[0]
                wait(pe, bank_free[n % 4], l * BPL + n // 4)
                return psum[:, 4 + n % 4, :]

            def full(ins, name):
                ins.then_inc(bank_full[uses[name] % 4], 1)

            def gemm(l, u, p0=0, p1=None, needs=None):
                hi, lo = act[u.act]
                if p0 == 0:
                    wait(pe, pair_free[u.n % 2], l * (len(units) // 2) + u.n // 2)
                for p in range(p0, u.pieces if p1 is None else p1):
                    g = u.first + p
                    s = g % RING
                    pe.wait_ge(lo_ready, l * PIECES + g + 1)
                    for i in range(2):
                        kt = 2 * p + i
                        for name in (needs(kt) if needs else ()):
                            wait_freed(pe, l, name)
                        a, z = kt == 0, kt == u.tiles - 1
                        if u.form == "tok":
                            for t in range(NT):
                                o, tt = pair(u)[:, t, 0:u.width], slice(t * P, t * P + P)
                                wh, wl = w_hi[:, s, i, 0:u.width], w_lo[:, s, i, 0:u.width]
                                mm(o, hi[:, kt, tt], wh, start=a, stop=False)
                                mm(o, hi[:, kt, tt], wl, start=False, stop=False)
                                last = mm(o, lo[:, kt, tt], wh, start=False, stop=z)
                        else:
                            for c in range(u.width // P):
                                o, cc = pair_ch(u)[:, c, :], slice(c * P, c * P + P)
                                mm(o, w_hi[:, s, i, cc], hi[:, kt, :], start=a and c % 2 == 0, stop=False,
                                   skip_group_check=True)
                                mm(o, w_hi[:, s, i, cc], lo[:, kt, :], start=False, stop=False,
                                   skip_group_check=True)
                                last = mm(o, w_lo[:, s, i, cc], hi[:, kt, :], start=False, stop=z,
                                          skip_group_check=True)
                    last.then_inc(piece_done, 1)
                    last_piece[0] = g

            def norm_tile(l, w, kt):
                if kt % 8 == 0:
                    pe.wait_ge(*at("xs_ready", l, 4 * w + 2 + kt // 4))
                b = take(l, ("norm", w, kt))
                for t in range(NT):
                    last = tp(b[:, t * P:t * P + P], xs[:, t, kt * P:kt * P + P], ident)
                full(last, ("norm", w, kt))

            def norm_and_gemm(l, w, u):
                for kt in range(4):
                    norm_tile(l, w, kt)
                for p in range(u.pieces):
                    gemm(l, u, p, p + 1, needs=lambda kt: [("norm", w, kt)])
                    for kt in (2 * p + 4, 2 * p + 5):
                        if kt < KT:
                            norm_tile(l, w, kt)

            def gdn_group(l, g):
                combos = [(t, h) for t in range(NT) for h in range(GH)]
                pe.wait_ge(*at("sqs", l, 2 * g + 2))
                b = take(l, ("ssq", g))
                for s, sq in enumerate((sqq, sqk)):
                    sqv = sq.rearrange("p (h t) n -> p h (t n)", h=GH)
                    for t, h in combos:
                        c = s * NC + t * GH + h
                        last = mm(b[:, c:c + 1], sqv[:, h, t * P:t * P + P], ones[:, 0:1])
                full(last, ("ssq", g))
                pe.wait_ge(*at("silu_out", l, 3 * g + 3))
                for name, src in (("k", k_t), ("v", v_t)):
                    for t in range(NT):
                        b = take(l, (name, g, t))
                        for h in range(GH):
                            last = tp(b[:, h * P:h * P + P], src[:, h, t * P:t * P + P], ident)
                        full(last, (name, g, t))
                if g == 0:
                    pe.wait_ge(*at("gate_g", l, 1))
                    b = take(l, "gcum")
                    full(mm(b[:, 0:12], cst("tri"), gate), "gcum")
                pe.wait_ge(*at("trig_ready", l, g + 1))
                for t in range(NT):
                    b = take(l, ("grow", g, t))
                    full(mm(b[:, 0:GH * P], ones, trig[:, t * GH:t * GH + GH, :]), ("grow", g, t))
                for t in range(NT):
                    wait_freed(pe, l, ("k", g, t))
                    b = take(l, ("kn", g, t))
                    for h in range(GH):
                        last = tp(b[:, h * P:h * P + P], kn[:, t * GH + h, :], ident)
                    full(last, ("kn", g, t))
                for t in range(NT):
                    wait_freed(pe, l, ("kn", g, t))
                    b = take(l, ("kk", g, t))
                    for h in range(GH):
                        i = t * GH + h
                        last = mm(b[:, h * P:h * P + P], kn_t[:, i, :], kn_t[:, i, :])
                    full(last, ("kk", g, t))
                for t in range(NT):
                    b = take(l, ("kq", g, t))
                    for h in range(GH):
                        last = mm(b[:, h * P:h * P + P], kn_t[:, t * GH + h, :], q_t[g][:, h, t * P:t * P + P])
                    full(last, ("kq", g, t))
                for lev in range(LEVELS):
                    pe.wait_ge(*at("off_ready", l, g * LEVELS + lev + 1))
                    for t in range(NT):
                        if lev:
                            wait_freed(pe, l, ("U", g, lev - 1, t))
                        b = take(l, ("R", g, lev, t))
                        for h in range(GH):
                            i = t * GH + h
                            last = mm(b[:, h * P:h * P + P], aoff[:, i, :], umat[:, i, :] if lev else ident)
                        full(last, ("R", g, lev, t))
                    if lev == 0:
                        for t in range(NT):
                            uses[("U", g, 0, t)] = uses[("R", g, 0, t)]
                            piece_before[("U", g, 0, t)] = last_piece[0]
                        continue
                    for t in range(NT):
                        wait_freed(pe, l, ("R", g, lev, t))
                        if lev == 1:
                            pe.wait_ge(*at("t_ready", l, g + 1))
                        else:
                            wait_freed(pe, l, ("T", g, lev - 1, t))
                        b = take(l, ("U", g, lev, t))
                        for h in range(GH):
                            i = t * GH + h
                            last = mm(b[:, h * P:h * P + P], tmat[:, i, :], rmat[:, i, :])
                        full(last, ("U", g, lev, t))
                        if lev < LEVELS - 1:
                            b = take(l, ("T", g, lev, t))
                            for h in range(GH):
                                i = t * GH + h
                                last = mm(b[:, h * P:h * P + P], rmat[:, i, :], tmat[:, i, :])
                            full(last, ("T", g, lev, t))

            def gdn_scan(l, g):
                wait_freed(pe, l, ("v", g, 0))
                wait_freed(pe, l, ("U", g, LEVELS - 1, 0))
                b = take(l, ("vn0", g))
                for h in range(GH):
                    last = mm(b[:, h * P:h * P + P], umat[:, h, :], vb[:, h, :])
                full(last, ("vn0", g))
                wait_freed(pe, l, ("v", g, 1))
                wait_freed(pe, l, ("U", g, LEVELS - 1, 1))
                pe.wait_ge(*at("ksc_ready", l, 2 * g + 2))
                b = take(l, ("w1", g))
                for h in range(GH):
                    last = mm(b[:, h * P:h * P + P], ksc[:, GH + h, :], umat[:, GH + h, :])
                full(last, ("w1", g))
                wait_freed(pe, l, ("vn0", g))
                b = take(l, ("s1", g))
                for h in range(GH):
                    last = mm(b[:, h * P:h * P + P], ksc[:, h, :], vn[:, h, :])
                full(last, ("s1", g))
                for t in range(NT):
                    wait_freed(pe, l, ("kq", g, t))
                b = take(l, ("o0", g))
                for h in range(GH):
                    last = mm(b[:, h * P:h * P + P], dec_t[:, h, :], vn[:, h, :])
                full(last, ("o0", g))
                wait_freed(pe, l, ("w1", g))
                wait_freed(pe, l, ("s1", g))
                b = take(l, ("vn1", g))
                for h in range(GH):
                    mm(b[:, h * P:h * P + P], umat[:, GH + h, :], vb[:, GH + h, :], stop=False)
                    last = mm(b[:, h * P:h * P + P], w1[:, h, :], s1[:, h, :], start=False)
                full(last, ("vn1", g))
                b = take(l, ("qs", g))
                for h in range(GH):
                    last = mm(b[:, h * P:h * P + P], q_t[g][:, h, P:2 * P], s1[:, h, :])
                full(last, ("qs", g))
                wait_freed(pe, l, ("vn1", g))
                b = take(l, ("o1", g))
                for h in range(GH):
                    last = mm(b[:, h * P:h * P + P], dec_t[:, GH + h, :], vn[:, GH + h, :])
                full(last, ("o1", g))

            def gdn_out(l, g):
                pe.wait_ge(*at("o_ready", l, g + 1))
                for h in range(GH):
                    b = take(l, ("oT", g, h))
                    for t in range(NT):
                        last = tp(b[:, t * P:t * P + P], obuf[:, t * GH + h, :], ident)
                    full(last, ("oT", g, h))

            def gate_weights(l):
                pe.wait_ge(*at("gate_w", l, 1))
                b = take(l, "sgw")
                for i in range(SG_GROUPS):
                    last = tp(b[:, i * P:i * P + P], sgw[:, i, :], ident)
                full(last, "sgw")

            def gate_mix(l):
                wait_freed(pe, l, "sgw")
                for t in range(NT):
                    pe.wait_ge(*at("gate_v", l, t + 1))
                    b = take(l, ("sg", t))
                    for i in range(SG_GROUPS):
                        last = mm(b[:, i * P:i * P + P], sgw_t[:, i, :], zv[:, t, i * P:i * P + P])
                    full(last, ("sg", t))

            def gate_out(l):
                for t in range(NT):
                    wait_freed(pe, l, ("sg", t))
                for i in range(SG_GROUPS):
                    b = take(l, ("bT", i))
                    for t in range(NT):
                        last = tp(b[:, t * P:t * P + P], zu[:, t, i * P:i * P + P], ident)
                    full(last, ("bT", i))

            def idx_transposes(l):
                pe.wait_ge(*at("rope_done", l, 3))
                b = take(l, "ikT")
                for t in range(NT):
                    last = tp(b[:, t * P:t * P + P], ik2[:, t, :], ident)
                full(last, "ikT")
                for t in range(NT):
                    for half in range(2):
                        b = take(l, ("iqT", t, half))
                        for i in range(4):
                            c = (half * 4 + i) * P
                            last = tp(b[:, i * P:i * P + P], ibuf[:, t, c:c + P], ident)
                        full(last, ("iqT", t, half))

            def idx_scores(l, t):
                width = (t + 1) * P
                per = COL // width
                wait_freed(pe, l, "ikT")
                for half in range(2):
                    wait_freed(pe, l, ("iqT", t, half))
                for n in range(IDX_HEADS // per):
                    b = take(l, ("score", t, n))
                    for i in range(per):
                        h = score_head(n, i, per)
                        r = slice((h % 2) * 64, (h % 2) * 64 + 64)
                        last = mm(b[:, i * width:(i + 1) * width], iq_t[r, t, h // 2, :], ik_t[r, 0:width])
                    full(last, ("score", t, n))

            def att_transposes(l):
                pe.wait_ge(*at("rope_done", l, 5))
                b = take(l, "ckT")
                for t in range(NT):
                    last = tp(b[:, t * P:t * P + P], cbuf[:, t, D_C:D_C + P], ident)
                full(last, "ckT")
                for n in range(3):
                    b = take(l, ("cqT", n))
                    for i in range(2):
                        h = 2 * n + i
                        for t in range(NT):
                            c = i * SEQ + t * P
                            last = tp(b[:, c:c + P], cbuf[:, t, h * P:h * P + P], ident)
                    full(last, ("cqT", n))

            def att_logits(l, t):
                width = (t + 1) * P
                per = 3 if t == 0 else 2
                wait_freed(pe, l, "ckT")
                for n in range(3):
                    wait_freed(pe, l, ("cqT", n))
                for n in range(SA_HEADS // per):
                    b = take(l, ("logit", t, n))
                    for i in range(per):
                        h = n * per + i
                        last = mm(b[:, i * width:(i + 1) * width], cq_t[:, h, t * P:t * P + P], ck_t[:, 0:width])
                    full(last, ("logit", t, n))

            def att_out(l, t):
                pe.wait_ge(*at("att_p", l, t + 1))
                for s in range(t + 1):
                    for n in range(2):
                        b = take(l, ("pT", t, s, n))
                        for i in range(GH):
                            last = tp(b[:, i * P:i * P + P], logit[:, n * GH + i, s * P:s * P + P], ident)
                        full(last, ("pT", t, s, n))
                for n in range(2):
                    for s in range(t + 1):
                        wait_freed(pe, l, ("pT", t, s, n))
                    b = take(l, ("aoT", t, n))
                    for i in range(GH):
                        for s in range(t + 1):
                            last = mm(b[:, i * P:i * P + P], cbuf[:, s, D_C + P:D_C + 2 * P],
                                      p_t[:, n * GH + i, s, :], start=s == 0, stop=s == t)
                    full(last, ("aoT", t, n))

            def mem_tile(l, kt):
                if kt % 8 == 0:
                    pe.wait_ge(*at("mem_scaled", l, 2 + kt // 4))
                b = take(l, ("mem", kt))
                for t in range(NT):
                    last = tp(b[:, t * P:t * P + P], mem_x[:, t, kt * P:kt * P + P], ident)
                full(last, ("mem", kt))

            def cross_logits(l):
                wait_pair_freed(pe, l, U["KM"])
                wait_pair_freed(pe, l, U["QM"])
                for t in range(NT):
                    for n in range(2):
                        b = take(l, ("xlogit", t, n))
                        for i in range(2):
                            h = 2 * n + i
                            last = mm(b[:, i * SEQ:(i + 1) * SEQ], qm_t[:, h, t * P:t * P + P], km_t[:, h, :])
                        full(last, ("xlogit", t, n))

            def cross_out(l):
                for t in range(NT):
                    pe.wait_ge(*at("xp_ready", l, t + 1))
                    for s in range(NT):
                        b = take(l, ("xpT", t, s))
                        for h in range(MEM_HEADS):
                            last = tp(b[:, h * P:h * P + P], xlogit[:, t, h, s * P:s * P + P], ident)
                        full(last, ("xpT", t, s))
                wait_pair_freed(pe, l, U["VM"])
                for t in range(NT):
                    for s in range(NT):
                        wait_freed(pe, l, ("xpT", t, s))
                for h in range(MEM_HEADS):
                    b = take(l, ("xo", h))
                    for s in range(NT):
                        last = mm(b[:, 0:SEQ], vm[:, s, h * P:h * P + P], xp_t[:, h, s, :], start=s == 0, stop=s == 1)
                    full(last, ("xo", h))

            def hidden(l, q, j):
                pe.wait_ge(*at("h_sq_ready", l, q * 4 + j + 1))
                for half in range(2):
                    b = take(l, ("hT", q, j, half))
                    for i in range(2):
                        for t in range(NT):
                            c = t * COL + (2 * half + i) * P
                            o = (i * NT + t) * P
                            last = tp(b[:, o:o + P], h_sq[:, j % 2, c:c + P], ident)
                    full(last, ("hT", q, j, half))

            def layer(l):
                cnt[0], last_piece[0] = 0, -1
                if l == 0:
                    pe.wait_ge(start_sem, 48)
                pe.wait_ge(*at("params_landed", l, 9 * 16))
                for i in range(2):
                    b = take(l, ("par", i))
                    n = PAR_ROWS[i]
                    full(tp(b[:, 0:n], par_rows[0:n, i, :], ident[0:n, 0:n]), ("par", i))
                norm_and_gemm(l, 0, U["B1"])
                gate_weights(l)
                gemm(l, U["B0"])
                gemm(l, U["I0"])
                gate_mix(l)
                gemm(l, U["I1"])
                gate_out(l)
                gemm(l, U["I2"])
                gemm(l, U["C0"])
                idx_transposes(l)
                gemm(l, U["C1"])
                idx_scores(l, 0)
                gemm(l, U["Q0"], 0, 4)
                idx_scores(l, 1)
                gemm(l, U["Q0"], 4)
                att_transposes(l)
                gemm(l, U["K0"])
                att_logits(l, 0)
                gemm(l, U["V0"])
                att_out(l, 0)
                att_logits(l, 1)
                gemm(l, U["Z1"])
                att_out(l, 1)
                gemm(l, U["Q1"])
                gdn_group(l, 0)
                gemm(l, U["K1"])
                gdn_scan(l, 0)
                gemm(l, U["V1"])
                gemm(l, U["Z0"])
                gdn_out(l, 0)
                gdn_group(l, 1)
                gdn_scan(l, 1)
                gdn_out(l, 1)

                def mixed(kt):
                    if kt < 6:
                        return [("oT", kt // GH, kt % GH)]
                    if kt < 10:
                        return [("bT", kt - 6)]
                    return [("aoT", t, (kt - 10) // GH) for t in range(NT)]

                gemm(l, U["O0"], needs=mixed)
                gemm(l, U["O1"])
                for kt in range(KT):
                    mem_tile(l, kt)
                    if kt == 7:
                        gemm(l, U["O2"])
                gemm(l, U["O3"])
                gemm(l, U["KM"], needs=lambda kt: [("mem", kt)])
                gemm(l, U["VM"])
                norm_and_gemm(l, 1, U["QM"])
                cross_logits(l)
                cross_out(l)
                gemm(l, U["OM0"], needs=lambda kt: [("xo", kt)])
                for j in range(1, 4):
                    gemm(l, U[f"OM{j}"])
                for q in range(4):
                    if q == 0:
                        norm_and_gemm(l, 2, U["U00"])
                    else:
                        gemm(l, U[f"U{q}0"])
                    for j in range(1, 4):
                        gemm(l, U[f"U{q}{j}"], 0, 4)
                        hidden(l, q, j - 1)
                        gemm(l, U[f"U{q}{j}"], 4)
                    need = lambda kt, q=q: [("hT", q, kt // 4, (kt % 4) // 2)]
                    gemm(l, U[f"D{q}0"], 0, 4, needs=need)
                    hidden(l, q, 3)
                    gemm(l, U[f"D{q}0"], 4, needs=need)
                    for j in range(1, 4):
                        gemm(l, U[f"D{q}{j}"])
                while cnt[0] % 4:
                    b = take(l, ("pad", cnt[0]))
                    full(mm(b[:, 0:1], ident, ones[:, 0:1]), ("pad", cnt[0] - 1))
                assert cnt[0] == USES, cnt[0]

            for l in range(DEPTH):
                layer(l)

        assert not any(n[0] == "pad" for n in uses), uses

        @block.sync
        def _(sp):
            sp.dma_start(const[:], consts).then_inc(start_sem, 16)
            for t in range(NT):
                sp.dma_start(x_res[:, t, :], x[0, t * P:t * P + P, :]).then_inc(start_sem, 16)

            def params(l):
                if l > 0:
                    sp.wait_ge(*at("gate_g", l - 1, 1))
                land = sems["params_landed"]
                for i, v in enumerate((ln_mix, ln_cross, ln_mem, ln_mlp)):
                    sp.dma_start(par_rows[16 * i:16 * i + 16, 0, :], v[l].rearrange("(k p) -> k p", p=P)).then_inc(land, 16)
                sp.dma_start(par_rows[64:68, 0, :], sg_b[l]).then_inc(land, 16)
                sp.dma_start(par_rows[68:69, 0, :], gdn_norm[l:l + 1, :]).then_inc(land, 16)
                sp.dma_start(par_rows[0:72, 1, :], conv_w[l].rearrange("j (c p) -> (j c) p", p=P)).then_inc(land, 16)
                sp.dma_start(al, a_log[l:l + 1, :].to_broadcast([P, GDN_HEADS])).then_inc(land, 16)
                sp.dma_start(dtb, dt_bias[l:l + 1, :].to_broadcast([P, GDN_HEADS])).then_inc(land, 16)

            def rows(l):
                if l > 0:
                    sp.wait_ge(*at("gate_v", l - 1, 2))
                    wait_full(sp, l - 1, "sgw")
                rows_landed = sems["rows_landed"]
                sp.dma_start(ln_rows[:, 0, :], sg_ln_g[l:l + 1, :].to_broadcast([P, D_B])).then_inc(rows_landed, 16)
                sp.dma_start(ln_rows[:, 1, :], sg_ln_b[l:l + 1, :].to_broadcast([P, D_B])).then_inc(rows_landed, 16)
                sp.dma_start(sgw[:], sg_w[l].rearrange("g t s -> t g s")).then_inc(rows_landed, 16)

            for l in range(DEPTH):
                params(l)
                for u in units:
                    if u.name == "B0":
                        rows(l)
                    if u.name == "O1":
                        wait_freed(sp, l, ("oT", 1, GH - 1))
                        for t in range(NT):
                            sp.dma_start(mem_x[:, t, :], mem[0, t * P:t * P + P, :]).then_inc(sems["mem_landed"], 16)
                    for p in range(u.pieces):
                        g = u.first + p
                        wait(sp, lo_ready, l * PIECES + g + 1 - RING)
                        r = u.r0 + 2 * p * P
                        src = matrices[u.mat][l, r:r + 2 * P, u.c0:u.c0 + u.width].rearrange("(k p) n -> p k n", p=P)
                        sp.dma_start(w_raw[:, g % RING, :, 0:u.width], src).then_inc(w_landed[g % RING], 16)
            sp.wait_ge(*at("h_sq_ready", DEPTH - 1, 16))
            sp.dma_start(fin_row, ln_final.rearrange("(a n) -> a n", a=1).to_broadcast([P, D_MODEL])).then_inc(fin_row_sem, 16)
            for t in range(NT):
                sp.wait_ge(fin_sem, t + 1)
                sp.dma_start(out[0, t * P:t * P + P, :], fin[:, t, :]).then_inc(out_sem, 16)
            sp.wait_ge(out_sem, 32)

        def each(a, n):
            return a.unsqueeze(1).to_broadcast([P, n, a.shape[-1]])

        def ci(t, g, h):
            return t * GDN_HEADS + g * GH + h

        @block.scalar
        def _(sc):
            act_fn = nc.scalar.activation
            chain = Chain(sc, "scalar_done", 0)
            nxt = [0]

            def ahead(l, piece):
                while nxt[0] <= min(piece + RING, PIECES - 1):
                    g = nxt[0]
                    nxt[0] += 1
                    u = [v for v in units if v.first <= g][-1]
                    s, w = g % RING, u.width
                    sc.wait_ge(w_landed[s], 16 * ((l * PIECES + g) // RING + 1))
                    wait(sc, piece_done, l * PIECES + g + 1 - RING)
                    act_fn(w_hi[:, s, :, 0:w], w_raw[:, s, :, 0:w], ACT.Copy).then_inc(hi_ready, 1)

            def reach(l, name):
                ahead(l, piece_before[name])
                wait_full(sc, l, name)
                return bank_of(name)

            def reach_unit(l, u):
                ahead(l, u.first + u.pieces - 1)
                wait_unit(sc, l, u)

            def copy_out(l, name, dst, n, scale=1.0, split=None):
                b = reach(l, name)[:, 0:n]
                if split:
                    b = b.rearrange("p (a b) -> p a b", b=split)
                free(act_fn(dst, b, ACT.Copy, scale=scale), name)

            def hi_part(l, name, dst, sig, scale=None):
                b = reach(l, name)[:, 0:int(np.prod(dst.shape[1:]))]
                if len(dst.shape) == 3:
                    b = b.rearrange("p (a b) -> p a b", b=dst.shape[2])
                if scale is None:
                    signal(act_fn(dst, b, ACT.Copy), sig)
                else:
                    signal(act_fn(dst, b, ACT.Identity, scale=scale), sig)

            def squares(l, j, t_base=0):
                for t in range(NT):
                    c = slice(j * COL, j * COL + COL)
                    signal(act_fn(xs[:, t, c], x_res[:, t, c], ACT.Square, accum_out=ssq[:, t * 4 + j:t * 4 + j + 1]),
                           "ssq_ready")

            def norm_hi(l, w, name, kt):
                hi_part(l, (("norm", w, kt) if w < 3 else ("mem", kt)), act["A"][0][:, kt, :], "act_hi",
                        scale=gain(name, kt))

            def gelu_units(l):
                reach_unit(l, U["B1"])
                for t in range(NT):
                    ins = act_fn(zv[:, t, :], pair(U["B1"])[:, t, :], ACT.Gelu_apprx_tanh, accum_out=mean[:, t:t + 1])
                    if t == NT - 1:
                        free_pair(ins, U["B1"])
                sc.wait_ge(*at("gate_nmean", l, 1))
                for t in range(NT):
                    signal(act_fn(sq_junk[:, t, :], zv[:, t, :], ACT.Square, bias=mean[:, t:t + 1],
                                  accum_out=rstd[:, t:t + 1]), "gate_var")
                reach_unit(l, U["B0"])
                free_pair(act_fn(zu, pair(U["B0"]), ACT.Gelu_apprx_tanh), U["B0"])

            def columns(l, u, dst):
                reach_unit(l, u)
                free_pair(act_fn(dst, pair(u)[:, :, 0:u.width], ACT.Copy), u)

            def conv_in(l, s, g):
                u = U[f"{'QKV'[s]}{g}"]
                reach_unit(l, u)
                n = 3 * g + s
                if n == 0:
                    sc.wait_ge(*at("rope_done", l, 5))
                    chain.run(act_fn(x_pad[:, :, 0:CONV_K - 1], const[:, 0:9].rearrange("p (a b) -> p a b", b=3),
                                     ACT.Copy, scale=0.0))
                else:
                    sc.wait_ge(*at("conv_out", l, n))
                free_pair(act_fn(x_pad[:, :, CONV_K - 1:], pair_ch(u)[:, 0:GH, :], ACT.Copy), u)

            def silu(l, s, g):
                sc.wait_ge(*at("conv_out", l, 3 * g + s + 1))
                d = (q_t[g], k_t, v_t)[s]
                signal(act_fn(d, d, ACT.Silu), "silu_out")

            def decays(l):
                reach_unit(l, U["Z1"])
                signal(act_fn(db.rearrange("p (t n) -> p t n", t=NT), pair(U["Z1"])[:, :, ZREST - 12:ZREST], ACT.Copy),
                       "db_ready")
                sc.wait_ge(*at("att_p", l, 2))
                free_pair(act_fn(zz[:, :, COL:], pair(U["Z1"])[:, :, 0:D_A - COL], ACT.Silu), U["Z1"])
                dbv = db.rearrange("p (t n) -> p t n", t=NT)
                sc.wait_ge(*at("db_ready", l, 1))
                signal(act_fn(beta.rearrange("p (t n) -> p t n", t=NT), dbv[:, :, 6:12], ACT.Exp, scale=-1.0), "beta_exp")
                signal(act_fn(eal, al, ACT.Exp), "eal_ready")
                sc.wait_ge(*at("abs_ready", l, 1))
                chain.link(l, act_fn(t_abs, t_abs, ACT.Exp, scale=-1.0))
                signal(act_fn(t_abs, t_abs, ACT.Ln, bias=ones[:, 0:1]), "dec_ln")

            def group_start(l, g):
                sc.wait_ge(*at("silu_out", l, 3 * g + 2))
                if g == 0:
                    wait_freed(sc, l, ("aoT", 1, 1))
                else:
                    reach(l, ("oT", g - 1, GH - 1))
                for src, dst in ((q_t[g], sqq), (k_t, sqk)):
                    signal(act_fn(dst.rearrange("p a b -> p (a b)"), src.rearrange("p a b -> p (a b)"), ACT.Square),
                           "sqs")

            def group_mid(l, g):
                sc.wait_ge(*at("beta_ready", l, 1))
                for t in range(NT):
                    b = reach(l, ("v", g, t))
                    for h in range(GH):
                        c = ci(t, g, h)
                        ins = act_fn(vb[:, t * GH + h, :], b[:, h * P:h * P + P], ACT.Identity, scale=beta[:, c:c + 1])
                    free(ins, ("v", g, t))
                if g == 0:
                    wait_freed(sc, l, "gcum")
                    signal(act_fn(eg, gcum, ACT.Exp), "eg_ready")
                ahead(l, piece_before[("grow", g, 1)])
                for t in range(NT):
                    wait_freed(sc, l, ("grow", g, t))
                    for h in range(GH):
                        i, c = t * GH + h, ci(t, g, h)
                        chain.run(act_fn(dec[:, i, :], dec[:, i, :], ACT.Exp, scale=-1.0, bias=gcum[:, c:c + 1]))
                        ins = act_fn(dec_t[:, i, :], dec_t[:, i, :], ACT.Exp, bias=ngcum[:, c:c + 1])
                        if h < GH - 1:
                            chain.run(ins)
                    signal(ins, "dec_val")
                sc.wait_ge(*at("kd_arg", l, g + 1))
                signal(act_fn(egl, glast, ACT.Exp), "egl_ready")
                for t in range(NT):
                    copy_out(l, ("kn", g, t), kn_t[:, t * GH:t * GH + GH, :], GH * P, split=P)

            def group_inverse(l, g):
                for lev in range(1, LEVELS):
                    for t in range(NT):
                        copy_out(l, ("R", g, lev, t), rmat[:, t * GH:t * GH + GH, :], GH * P, split=P)

            def group_scan(l, g):
                reach(l, ("U", g, LEVELS - 1, 1))
                sc.wait_ge(*at("beg_ready", l, 1))
                sc.wait_ge(*at("egl_ready", l, g + 1))
                for t, f in ((0, egl), (1, beg)):
                    for h in range(GH):
                        c = h if t == 0 else ci(1, g, h)
                        ins = act_fn(ksc[:, t * GH + h, :], kn[:, t * GH + h, :], ACT.Identity, scale=f[:, c:c + 1])
                        if h < GH - 1:
                            chain.run(ins)
                        else:
                            signal(ins, "ksc_ready")
                    if t == 0:
                        signal_pad = None
                copy_out(l, ("vn0", g), vn[:, 0:GH, :], GH * P, split=P)
                copy_out(l, ("w1", g), w1, GH * P, scale=-1.0, split=P)
                copy_out(l, ("s1", g), s1, GH * P, split=P)
                copy_out(l, ("vn1", g), vn[:, GH:, :], GH * P, split=P)
                b = reach(l, ("qs", g))
                for h in range(GH):
                    c = ci(1, g, h)
                    ins = act_fn(qs[:, h, :], b[:, h * P:h * P + P], ACT.Identity, scale=eg[:, c:c + 1])
                free(ins, ("qs", g))

            def group_out(l, g):
                ahead(l, piece_before[("oT", g, 0)])
                for h in range(GH):
                    hi_part(l, ("oT", g, h), act["B"][0][:, g * GH + h, :], "gdn_hi", scale=gain("gdn", 0))

            def relus(l, t):
                width = (t + 1) * P
                per = COL // width
                for n in range(IDX_HEADS // per):
                    k = n + (4 if t else 0)
                    name = ("score", t, n)
                    b = reach(l, name)
                    if k >= 2:
                        sc.wait_ge(*at("relu_used", l, k - 1))
                    free(act_fn(relu[:, k % 2, :], b, ACT.Relu), name)

            def att_softmax(l, t):
                width = (t + 1) * P
                ahead(l, piece_before[("logit", t, 2 if t else 1)])
                sc.wait_ge(*at("logits_ready", l, t + 1))
                for h in range(SA_HEADS):
                    signal(act_fn(logit[:, h, 0:width], logit[:, h, 0:width], ACT.Exp,
                                  bias=smax[:, t * 6 + h:t * 6 + h + 1], accum_out=ssum[:, t * 6 + h:t * 6 + h + 1]),
                           "att_exp")

            def att_values(l, t):
                ahead(l, piece_before[("pT", t, 0, 0)])
                for s in range(t + 1):
                    for n in range(2):
                        copy_out(l, ("pT", t, s, n), p_t[:, n * GH:n * GH + GH, s, :], GH * P, split=P)
                for n in range(2):
                    hi_part(l, ("aoT", t, n), act["B"][0][:, 10 + n * GH:10 + n * GH + GH, t * P:t * P + P], "att_hi")

            def layer(l):
                nxt[0] = 0
                if l > 0:
                    wait_freed(sc, l - 1, ("norm", 2, KT - 1))
                for i in range(2):
                    wait_full(sc, l, ("par", i))
                    n = PAR_ROWS[i]
                    free(act_fn(par[:, i, 0:n], bank_of(("par", i))[:, 0:n], ACT.Copy), ("par", i))
                wait_freed(sc, l, ("par", 1))
                for kt in range(KT):
                    norm_hi(l, 0, "ln_mix", kt)
                gelu_units(l)
                copy_out(l, "sgw", sgw_t.rearrange("p a b -> p (a b)") if False else sgw_t[:], SG_GROUPS * P, split=P)
                columns(l, U["I0"], ibuf[:, :, 0:COL])
                columns(l, U["I1"], ibuf[:, :, COL:2 * COL])
                for i in range(SG_GROUPS):
                    hi_part(l, ("bT", i), act["B"][0][:, 6 + i, :], "gate_hi")
                columns(l, U["I2"], ibuf[:, :, 2 * COL:])
                columns(l, U["C0"], cbuf[:, :, 0:COL])
                copy_out(l, "ikT", ik_t, SEQ)
                for t in range(NT):
                    for half in range(2):
                        copy_out(l, ("iqT", t, half), iq_t[:, t, 4 * half:4 * half + 4, :], COL, split=P)
                columns(l, U["C1"], cbuf[:, :, COL:])
                relus(l, 0)
                relus(l, 1)
                conv_in(l, 0, 0)
                copy_out(l, "ckT", ck_t, SEQ)
                for n in range(3):
                    copy_out(l, ("cqT", n), cq_t[:, 2 * n:2 * n + 2, :], COL, split=SEQ)
                silu(l, 0, 0)
                conv_in(l, 1, 0)
                silu(l, 1, 0)
                att_softmax(l, 0)
                conv_in(l, 2, 0)
                silu(l, 2, 0)
                att_values(l, 0)
                att_softmax(l, 1)
                decays(l)
                att_values(l, 1)
                conv_in(l, 0, 1)
                silu(l, 0, 1)
                group_start(l, 0)
                group_mid(l, 0)
                group_inverse(l, 0)
                conv_in(l, 1, 1)
                silu(l, 1, 1)
                group_scan(l, 0)
                conv_in(l, 2, 1)
                silu(l, 2, 1)
                reach_unit(l, U["Z0"])
                free_pair(act_fn(zz[:, :, 0:COL], pair(U["Z0"]), ACT.Silu), U["Z0"])
                group_out(l, 0)
                group_start(l, 1)
                group_mid(l, 1)
                group_inverse(l, 1)
                group_scan(l, 1)
                group_out(l, 1)
                for j in range(4):
                    ahead(l, U[f"O{j}"].first + 7)
                    wait_pair_freed(sc, l, U[f"O{j}"])
                    squares(l, j)
                    if j == 1:
                        sc.wait_ge(*at("mem_landed", l, 32))
                        for t in range(NT):
                            signal(act_fn(region(8192, NT, D_MODEL)[:, t, :], mem_x[:, t, :], ACT.Square,
                                          accum_out=ssq_mem[:, t:t + 1]), "mem_ssq")
                        for kt in range(8):
                            norm_hi(l, 3, "ln_mem", kt)
                    if j == 2:
                        for kt in range(8, KT):
                            norm_hi(l, 3, "ln_mem", kt)
                columns_ch(l, U["KM"], km_t)
                columns(l, U["VM"], vm)
                for kt in range(KT):
                    norm_hi(l, 1, "ln_cross", kt)
                columns_ch(l, U["QM"], qm_t)
                for t in range(NT):
                    ahead(l, piece_before[("xlogit", t, 1)])
                    sc.wait_ge(*at("xlog_ready", l, t + 1))
                    for h in range(MEM_HEADS):
                        c = t * MEM_HEADS + h
                        signal(act_fn(xlogit[:, t, h, :], xlogit[:, t, h, :], ACT.Exp, bias=xmax[:, c:c + 1],
                                      accum_out=xsum[:, c:c + 1]), "xexp")
                for t in range(NT):
                    for s in range(NT):
                        copy_out(l, ("xpT", t, s), xp_t[:, :, s, t * P:t * P + P], COL, split=P)
                for h in range(MEM_HEADS):
                    hi_part(l, ("xo", h), act["B"][0][:, h, :], "xat_hi")
                for j in range(4):
                    ahead(l, U[f"OM{j}"].first + 1)
                    wait_pair_freed(sc, l, U[f"OM{j}"])
                    squares(l, j)
                for kt in range(KT):
                    norm_hi(l, 2, "ln_mlp", kt)
                for q in range(4):
                    for j in range(4):
                        u = U[f"U{q}{j}"]
                        n = q * 4 + j
                        if j:
                            hidden_hi(l, q, j - 1)
                        reach_unit(l, u)
                        if n >= 2:
                            sc.wait_ge(*at("h_sq_ready", l, n - 1))
                        free_pair(act_fn(h_relu[:, j % 2, :].rearrange("p (a b) -> p a b", b=COL), pair(u), ACT.Relu), u)
                    hidden_hi(l, q, 3)
                    if q == 3:
                        for j in range(4):
                            ahead(l, U[f"D{q}{j}"].first + 7)
                            wait_pair_freed(sc, l, U[f"D{q}{j}"])
                            squares(l, j)
                ahead(l, PIECES)

            def hidden_hi(l, q, j):
                for half in range(2):
                    hi_part(l, ("hT", q, j, half), act["B"][0][:, 4 * j + 2 * half:4 * j + 2 * half + 2, :], "ffn_hi")

            def columns_ch(l, u, dst):
                reach_unit(l, u)
                free_pair(act_fn(dst, pair_ch(u), ACT.Copy), u)

            sc.wait_ge(start_sem, 48)
            for j in range(4):
                squares(0, j)
            for l in range(DEPTH):
                layer(l)

        @block.vector
        def _(dve):
            V = nc.vector
            chain = Chain(dve, "vector_done", 0)
            nxt = [0]

            def ahead(l, piece):
                while nxt[0] <= min(piece + RING - 1, PIECES - 1):
                    g = nxt[0]
                    nxt[0] += 1
                    u = [v for v in units if v.first <= g][-1]
                    s, w = g % RING, u.width
                    dve.wait_ge(hi_ready, l * PIECES + g + 1)
                    V.tensor_tensor(w_lo[:, s, :, 0:w], w_raw[:, s, :, 0:w], w_hi[:, s, :, 0:w].bitcast(F32),
                                    ALU.subtract).then_inc(lo_ready, 1)

            def reach(l, name):
                ahead(l, piece_before[name])
                wait_full(dve, l, name)
                return bank_of(name)

            def reach_unit(l, u):
                ahead(l, u.first + u.pieces - 1)
                wait_unit(dve, l, u)

            def link(l, ins):
                chain.link(l, ins)

            def rsqrt(l, n, dst):
                y, a, b = y_in[:, 0:n], y_a[:, 0:n], y_b[:, 0:n]
                link(l, V.tensor_scalar(a.bitcast(I32), y.bitcast(I32), 1, None, ALU.logical_shift_right))
                link(l, V.tensor_scalar(dst.bitcast(I32), a.bitcast(I32), -1.0, float(0x5f3759df), ALU.mult, ALU.add))
                for _ in range(3):
                    link(l, V.tensor_tensor(a, dst, dst, ALU.mult))
                    link(l, V.scalar_tensor_tensor(out=b, in0=a, scalar=-0.5, in1=y, op0=ALU.mult, op1=ALU.mult))
                    link(l, V.scalar_tensor_tensor(out=dst, in0=b, scalar=1.5, in1=dst, op0=ALU.add, op1=ALU.mult))

            def lo_part(l, name, dst, hi, sig, count, scale=None):
                ahead(l, piece_before[name])
                dve.wait_ge(*at(sig, l, count))
                b = bank_of(name)[:, 0:int(np.prod(dst.shape[1:]))]
                if len(dst.shape) == 3:
                    b = b.rearrange("p (a b) -> p a b", b=dst.shape[2])
                hi = hi.bitcast(F32)
                if scale is None:
                    ins = V.tensor_tensor(dst, b, hi, ALU.subtract)
                else:
                    ins = V.scalar_tensor_tensor(out=dst, in0=b, scalar=scale, in1=hi, op0=ALU.mult, op1=ALU.subtract)
                free(ins, name)

            def norm_scale(l, w):
                dve.wait_ge(*at("ssq_ready", l, 8 * w))
                link(l, V.tensor_reduce(y_a[:, 0:2], ssq.rearrange("p (t j) -> p t j", j=4), AX.X, ALU.add))
                link(l, V.tensor_scalar(y_in[:, 0:2], y_a[:, 0:2], 1.0 / D_MODEL, EPS, ALU.mult, ALU.add))
                rsqrt(l, 2, r_norm)
                for half in range(2):
                    for t in range(NT):
                        c = slice(half * 1024, half * 1024 + 1024)
                        signal(V.tensor_scalar(xs[:, t, c], x_res[:, t, c], r_norm[:, t:t + 1], None, ALU.mult),
                               "xs_ready")

            def norm_lo(l, w, name, kt):
                use = ("norm", w, kt) if w < 3 else ("mem", kt)
                fill = {0: 0, 3: 1, 1: 2, 2: 3}[w]
                hi, lo = act["A"]
                lo_part(l, use, lo[:, kt, :], hi[:, kt, :], "act_hi", fill * KT + kt + 1, scale=gain(name, kt))

            def gate_norm(l):
                ahead(l, U["B1"].first + 7)
                wait_pair_freed(dve, l, U["B1"])
                signal(V.tensor_scalar(mean, mean, -1.0 / D_B, None, ALU.mult), "gate_nmean")
                dve.wait_ge(*at("gate_var", l, 2))
                link(l, V.tensor_scalar(y_in[:, 0:2], rstd, 1.0 / D_B, EPS, ALU.mult, ALU.add))
                rsqrt(l, 2, rstd)
                for t in range(NT):
                    signal(V.tensor_scalar(zv[:, t, :], zv[:, t, :], mean[:, t:t + 1], rstd[:, t:t + 1], ALU.add,
                                           ALU.mult), "gate_norm")

            def gate_apply(l):
                for t in range(NT):
                    b = reach(l, ("sg", t))
                    if t == 0:
                        wait_pair_freed(dve, l, U["B0"])
                    for i in range(SG_GROUPS):
                        c = slice(i * P, i * P + P)
                        ins = V.scalar_tensor_tensor(out=zu[:, t, c], in0=b[:, c], scalar=gain("sg_b", i),
                                                     in1=zu[:, t, c], op0=ALU.add, op1=ALU.mult)
                    free(ins, ("sg", t))

            def rope(l, buf, ta, tb, heads, half, cos, sin, n, units_):
                for u in units_:
                    ahead(l, u.first + u.pieces - 1)
                    wait_pair_freed(dve, l, u)
                w = heads * 2 * half

                def view(a, t):
                    return a[:, t, 0:w].rearrange("p (h a d) -> p h a d", a=2, d=half)

                for t in range(NT):
                    c = cst(cos, NT)[:, t, :].unsqueeze(1).unsqueeze(1).to_broadcast([P, heads, 2, half])
                    link(l, V.tensor_tensor(view(ta, t), view(buf, t), c, ALU.mult))
                    dve.wait_ge(*at("rope_b", l, n + t + 1))
                    x_, a_, b_ = view(buf, t), view(ta, t), view(tb, t)
                    chain.run(V.tensor_tensor(x_[:, :, 0, :], a_[:, :, 0, :], b_[:, :, 1, :], ALU.subtract))
                    signal(V.tensor_tensor(x_[:, :, 1, :], a_[:, :, 1, :], b_[:, :, 0, :], ALU.add), "rope_done")
                chain.settle(l)

            def index_rope(l):
                rope(l, ibuf, tmp_a, tmp_b, IDX_HEADS + 1, 32, "cos_i", "sin_i", 0, [U["I0"], U["I1"], U["I2"]])
                dve.wait_ge(*at("rope_done", l, 2))
                s = IDX_HEADS * IDX_DIM
                chain.run(V.tensor_scalar(iw.rearrange("p (t h) -> p t h", t=NT), ibuf[:, :, s + IDX_DIM:],
                                          IDX_HEADS ** -0.5 * IDX_DIM ** -0.5, None, ALU.mult))
                chain.run(V.tensor_copy(ik2[:, :, 0:64], ibuf[:, :, s:s + IDX_DIM]))
                signal(V.tensor_copy(ik2[:, :, 64:128], ibuf[:, :, s:s + IDX_DIM]), "rope_done")

            def scores(l, t):
                width = (t + 1) * P
                per = COL // width
                d = score[:, t, 0:width]
                for n in range(IDX_HEADS // per):
                    k = n + (4 if t else 0)
                    ahead(l, piece_before[("score", t, n)])
                    wait_freed(dve, l, ("score", t, n))
                    for i in range(per):
                        h = score_head(n, i, per)
                        src, wt = relu[:, k % 2, i * width:(i + 1) * width], iw[:, t * 16 + h:t * 16 + h + 1]
                        if h == 0:
                            chain.settle(l)
                            ins = V.tensor_scalar(d, src, wt, None, ALU.mult)
                        else:
                            ins = V.scalar_tensor_tensor(out=d, in0=src, scalar=wt, in1=d, op0=ALU.mult, op1=ALU.add)
                        if i < per - 1:
                            link(l, ins)
                        else:
                            signal(ins, "relu_used")
                            dve.wait_ge(*at("relu_used", l, k + 1))
                signal(V.tensor_copy(work[:, t, 0:width], d), "score_done")

            def topk(l, t):
                width = (t + 1) * P
                w = work[:, t, 0:width]
                dve.wait_ge(*at("masked", l, t + 1))
                for r in range(TOPK // 8):
                    m = max8[:, (t * 8 + r) * 8:(t * 8 + r) * 8 + 8]
                    link(l, V.max(m, w))
                    link(l, V.match_replace(w, m, w, TAKEN))
                signal(V.tensor_scalar(mbias[:, t, 0:width], w, -2e38, -OFF, ALU.is_gt, ALU.mult), "topk_done")

            def att_logits(l, t):
                width = (t + 1) * P
                per = 3 if t == 0 else 2
                if t == 0:
                    dve.wait_ge(*at("mask_ready", l, 1))
                else:
                    dve.wait_ge(*at("topk_done", l, 2))
                for n in range(SA_HEADS // per):
                    name = ("logit", t, n)
                    b = reach(l, name)
                    free(V.scalar_tensor_tensor(out=logit[:, n * per:(n + 1) * per, 0:width],
                                                in0=b[:, 0:per * width].rearrange("p (a b) -> p a b", b=width),
                                                scalar=SCALE, in1=each(mbias[:, t, 0:width], per),
                                                op0=ALU.mult, op1=ALU.add), name)
                for n in range(SA_HEADS // per):
                    wait_freed(dve, l, ("logit", t, n))
                c = slice(t * 6, t * 6 + 6)
                link(l, V.tensor_reduce(smax[:, c], logit[:, :, 0:width], AX.X, ALU.max))
                signal(V.tensor_scalar(smax[:, c], smax[:, c], -1.0, None, ALU.mult), "logits_ready")
                dve.wait_ge(*at("att_exp", l, 6 * (t + 1)))
                link(l, V.reciprocal(sinv[:, c], ssum[:, c]))
                for h in range(SA_HEADS):
                    ins = V.tensor_scalar(logit[:, h, 0:width], logit[:, h, 0:width], sinv[:, t * 6 + h:t * 6 + h + 1],
                                          None, ALU.mult)
                    if h < SA_HEADS - 1:
                        chain.run(ins)
                chain.settle(l)
                signal(ins, "att_p")

            def att_lo(l, t):
                hi, lo = act["B"]
                for n in range(2):
                    k, c = slice(10 + n * GH, 10 + n * GH + GH), slice(t * P, t * P + P)
                    lo_part(l, ("aoT", t, n), lo[:, k, c], hi[:, k, c], "att_hi", 2 * t + n + 1)

            def conv(l, s, g):
                n = 3 * g + s
                u = U[f"{'QKV'[s]}{g}"]
                ahead(l, u.first + u.pieces - 1)
                wait_pair_freed(dve, l, u)
                d = (q_t[g], k_t, v_t)[s]
                for j in reversed(range(CONV_K)):
                    for h in range(GH):
                        w = conv_tap(j, s * GDN_HEADS + g * GH + h)
                        src = x_pad[:, h, j:j + SEQ]
                        if j == CONV_K - 1:
                            ins = V.tensor_scalar(d[:, h, :], src, w, None, ALU.mult)
                        else:
                            ins = V.scalar_tensor_tensor(out=d[:, h, :], in0=src, scalar=w, in1=d[:, h, :],
                                                         op0=ALU.mult, op1=ALU.add)
                        if j == 0 and h == GH - 1:
                            signal(ins, "conv_out")
                        else:
                            chain.run(ins)
                    if j:
                        chain.settle(l)

            def decays(l):
                ahead(l, U["Z1"].first + 7)
                dve.wait_ge(*at("db_ready", l, 1))
                for t in range(NT):
                    chain.run(V.tensor_tensor(t_ln[:, t * 6:t * 6 + 6], db[:, t * 12:t * 12 + 6], dtb, ALU.add))
                chain.settle(l)
                signal(V.scalar_tensor_tensor(out=t_abs, in0=t_ln, scalar=-1.0, in1=t_ln, op0=ALU.mult, op1=ALU.max),
                       "abs_ready")
                dve.wait_ge(*at("beta_exp", l, 1))
                link(l, V.tensor_scalar(beta, beta, 1.0, None, ALU.add))
                signal(V.reciprocal(beta, beta), "beta_ready")
                dve.wait_ge(*at("dec_ln", l, 1))
                link(l, V.scalar_tensor_tensor(out=gate, in0=t_ln, scalar=0.0, in1=t_abs, op0=ALU.max, op1=ALU.add))
                dve.wait_ge(*at("eal_ready", l, 1))
                chain.run(V.scalar_tensor_tensor(out=gate[:, 0:6], in0=gate[:, 0:6], scalar=-1.0, in1=eal,
                                                 op0=ALU.mult, op1=ALU.mult))
                chain.settle(l)
                signal(V.scalar_tensor_tensor(out=gate[:, 6:12], in0=gate[:, 6:12], scalar=-1.0, in1=eal,
                                              op0=ALU.mult, op1=ALU.mult), "gate_g")

            def group_mid(l, g):
                b = reach(l, ("ssq", g))
                if g == 0:
                    wait_freed(dve, l, ("aoT", 1, 1))
                free(V.tensor_scalar(y_in[:, 0:12], b[:, 0:12], EPS, None, ALU.add), ("ssq", g))
                wait_freed(dve, l, ("ssq", g))
                rsqrt(l, 12, r_qk)
                for t in range(NT):
                    b = reach(l, ("k", g, t))
                    for h in range(GH):
                        i = t * GH + h
                        ins = V.tensor_scalar(kn[:, i, :], b[:, h * P:h * P + P], r_qk[:, NC + i:NC + i + 1], None,
                                              ALU.mult)
                        if h < GH - 1:
                            chain.run(ins)
                    free(ins, ("k", g, t))
                if g == 0:
                    b = reach(l, "gcum")
                    chain.run(V.tensor_scalar(ngcum, b[:, 0:12], -1.0, None, ALU.mult))
                    free(V.tensor_copy(gcum, b[:, 0:12]), "gcum")
                    wait_freed(dve, l, "gcum")
                    dve.wait_ge(*at("eg_ready", l, 1))
                    signal(V.tensor_tensor(beg, beta, eg, ALU.mult), "beg_ready")
                for t in range(NT):
                    b = reach(l, ("grow", g, t))[:, 0:GH * P].rearrange("p (a b) -> p a b", b=P)
                    r = slice(t * GH, t * GH + GH)
                    if t == 0:
                        chain.run(V.tensor_copy(glast.unsqueeze(2), b[:, :, P - 1:P]))
                    chain.run(V.tensor_tensor(dec[:, r, :], b, each(cst("strict"), GH), ALU.add))
                    free(V.tensor_tensor(dec_t[:, r, :], b, each(cst("incl"), GH), ALU.subtract), ("grow", g, t))
                chain.settle(l)
                signal(V.tensor_tensor(glast, glast, gcum[:, g * GH:g * GH + GH], ALU.subtract), "kd_arg")
                for t in range(NT):
                    b = reach(l, ("kk", g, t))
                    dve.wait_ge(*at("dec_val", l, 2 * g + t + 1))
                    for h in range(GH):
                        i, c = t * GH + h, ci(t, g, h)
                        ins = V.scalar_tensor_tensor(out=amat[:, i, :], in0=b[:, h * P:h * P + P],
                                                     scalar=beta[:, c:c + 1], in1=dec[:, i, :], op0=ALU.mult,
                                                     op1=ALU.mult)
                        if h < GH - 1:
                            chain.run(ins)
                    free(ins, ("kk", g, t))
                for t in range(NT):
                    b = reach(l, ("kq", g, t))[:, 0:GH * P].rearrange("p (a b) -> p a b", b=P)
                    r = slice(t * GH, t * GH + GH)
                    free(V.tensor_tensor(dec_t[:, r, :], b, dec_t[:, r, :], ALU.mult), ("kq", g, t))

            def group_inverse(l, g):
                dve.wait_ge(*at("off_ready", l, g * LEVELS + 1))
                signal(V.tensor_tensor(tmat, each(ident, NC), aoff, ALU.subtract), "t_ready")
                for t in range(NT):
                    b = reach(l, ("R", g, 0, t))[:, 0:GH * P].rearrange("p (a b) -> p a b", b=P)
                    free(V.tensor_tensor(umat[:, t * GH:t * GH + GH, :], each(ident, GH), b, ALU.subtract), ("R", g, 0, t))
                dve.wait_ge(*at("t_ready", l, g + 1))
                for lev in range(1, LEVELS):
                    for t in range(NT):
                        r = slice(t * GH, t * GH + GH)
                        for name, m in (("U", umat), ("T", tmat)):
                            if name == "T" and lev == LEVELS - 1:
                                continue
                            if lev > 1 or name == "U":
                                wait_freed(dve, l, (name, g, lev - 1, t))
                            b = reach(l, (name, g, lev, t))[:, 0:GH * P].rearrange("p (a b) -> p a b", b=P)
                            free(V.tensor_tensor(m[:, r, :], m[:, r, :], b, ALU.subtract), (name, g, lev, t))

            def group_scan(l, g):
                b = reach(l, ("o0", g))[:, 0:GH * P].rearrange("p (a b) -> p a b", b=P)
                free(V.tensor_copy(obuf[:, 0:GH, :], b), ("o0", g))
                b = reach(l, ("o1", g))[:, 0:GH * P].rearrange("p (a b) -> p a b", b=P)
                wait_freed(dve, l, ("qs", g))
                free(V.tensor_tensor(obuf[:, GH:, :], b, qs, ALU.add), ("o1", g))
                wait_freed(dve, l, ("o0", g))
                wait_freed(dve, l, ("o1", g))
                link(l, V.tensor_tensor(rmat, obuf, obuf, ALU.mult))
                link(l, V.tensor_reduce(y_b[:, 0:NC], rmat, AX.X, ALU.add))
                link(l, V.tensor_scalar(o_c, r_qk[:, 0:NC], SCALE, None, ALU.mult))
                link(l, V.tensor_tensor(y_a[:, 0:NC], o_c, o_c, ALU.mult))
                link(l, V.scalar_tensor_tensor(out=y_in[:, 0:NC], in0=y_b[:, 0:NC], scalar=1.0 / HEAD,
                                               in1=y_a[:, 0:NC], op0=ALU.mult, op1=ALU.mult))
                link(l, V.tensor_scalar(y_in[:, 0:NC], y_in[:, 0:NC], EPS, None, ALU.add))
                rsqrt(l, NC, r_o)
                link(l, V.tensor_tensor(o_f, o_c, r_o, ALU.mult))

            def group_gate(l, g):
                for name in ("Z0", "Z1"):
                    ahead(l, U[name].first + 7)
                    wait_pair_freed(dve, l, U[name])
                for i in range(NC):
                    t, h = i // GH, g * GH + i % GH
                    ins = V.scalar_tensor_tensor(out=obuf[:, i, :], in0=obuf[:, i, :], scalar=o_f[:, i:i + 1],
                                                 in1=zz[:, t, h * P:h * P + P], op0=ALU.mult, op1=ALU.mult)
                    if i < NC - 1:
                        chain.run(ins)
                chain.settle(l)
                signal(ins, "o_ready")

            def group_out(l, g):
                hi, lo = act["B"]
                for h in range(GH):
                    k = g * GH + h
                    lo_part(l, ("oT", g, h), lo[:, k, :], hi[:, k, :], "gdn_hi", k + 1, scale=gain("gdn", 0))

            def residual(l, u, j):
                reach_unit(l, u)
                c = slice(j * COL, j * COL + COL)
                free_pair(V.tensor_tensor(x_res[:, :, c], x_res[:, :, c], pair(u), ALU.add), u)

            def hidden_lo(l, q, j):
                hi, lo = act["B"]
                for half in range(2):
                    k = slice(4 * j + 2 * half, 4 * j + 2 * half + 2)
                    lo_part(l, ("hT", q, j, half), lo[:, k, :], hi[:, k, :], "ffn_hi", (q * 4 + j) * 2 + half + 1)

            def layer(l):
                nxt[0] = 0
                norm_scale(l, 0)
                wait_freed(dve, l, ("par", 1))
                for kt in range(KT):
                    norm_lo(l, 0, "ln_mix", kt)
                gate_norm(l)
                gate_apply(l)
                hi, lo = act["B"]
                for i in range(SG_GROUPS):
                    lo_part(l, ("bT", i), lo[:, 6 + i, :], hi[:, 6 + i, :], "gate_hi", i + 1)
                index_rope(l)
                rope(l, cbuf, rope_a, rope_b, SA_HEADS + 1, 64, "cos_h", "sin_h", 2, [U["C0"], U["C1"]])
                scores(l, 0)
                scores(l, 1)
                topk(l, 0)
                conv(l, 0, 0)
                topk(l, 1)
                conv(l, 1, 0)
                att_logits(l, 0)
                conv(l, 2, 0)
                att_lo(l, 0)
                att_logits(l, 1)
                decays(l)
                att_lo(l, 1)
                conv(l, 0, 1)
                group_mid(l, 0)
                group_inverse(l, 0)
                conv(l, 1, 1)
                group_scan(l, 0)
                conv(l, 2, 1)
                group_gate(l, 0)
                group_out(l, 0)
                group_mid(l, 1)
                group_inverse(l, 1)
                group_scan(l, 1)
                group_gate(l, 1)
                group_out(l, 1)
                for j in range(4):
                    residual(l, U[f"O{j}"], j)
                    if j == 1:
                        dve.wait_ge(*at("mem_ssq", l, 2))
                        link(l, V.tensor_scalar(y_in[:, 0:2], ssq_mem, 1.0 / D_MODEL, EPS, ALU.mult, ALU.add))
                        rsqrt(l, 2, r_norm)
                        for half in range(2):
                            for t in range(NT):
                                c = slice(half * 1024, half * 1024 + 1024)
                                signal(V.tensor_scalar(mem_x[:, t, c], mem_x[:, t, c], r_norm[:, t:t + 1], None,
                                                       ALU.mult), "mem_scaled")
                    if j in (1, 2):
                        for kt in range(8 * j - 8, 8 * j):
                            norm_lo(l, 3, "ln_mem", kt)
                norm_scale(l, 1)
                for kt in range(KT):
                    norm_lo(l, 1, "ln_cross", kt)
                for t in range(NT):
                    for n in range(2):
                        b = reach(l, ("xlogit", t, n)).rearrange("p (a b) -> p a b", b=MEM_LEN)
                        free(V.tensor_scalar(xlogit[:, t, 2 * n:2 * n + 2, :], b, SCALE, None, ALU.mult),
                             ("xlogit", t, n))
                    for n in range(2):
                        wait_freed(dve, l, ("xlogit", t, n))
                    c = slice(t * 4, t * 4 + 4)
                    link(l, V.tensor_reduce(xmax[:, c], xlogit[:, t, :, :], AX.X, ALU.max))
                    signal(V.tensor_scalar(xmax[:, c], xmax[:, c], -1.0, None, ALU.mult), "xlog_ready")
                for t in range(NT):
                    c = slice(t * 4, t * 4 + 4)
                    dve.wait_ge(*at("xexp", l, 4 * t + 4))
                    link(l, V.reciprocal(xinv[:, c], xsum[:, c]))
                    for h in range(MEM_HEADS):
                        ins = V.tensor_scalar(xlogit[:, t, h, :], xlogit[:, t, h, :],
                                              xinv[:, t * 4 + h:t * 4 + h + 1], None, ALU.mult)
                        if h < MEM_HEADS - 1:
                            chain.run(ins)
                    chain.settle(l)
                    signal(ins, "xp_ready")
                for h in range(MEM_HEADS):
                    lo_part(l, ("xo", h), lo[:, h, :], hi[:, h, :], "xat_hi", h + 1)
                for j in range(4):
                    residual(l, U[f"OM{j}"], j)
                norm_scale(l, 2)
                for kt in range(KT):
                    norm_lo(l, 2, "ln_mlp", kt)
                for q in range(4):
                    for j in range(3):
                        hidden_lo(l, q, j)
                    hidden_lo(l, q, 3)
                    for j in range(4):
                        residual(l, U[f"D{q}{j}"], j)
                ahead(l, PIECES)

            for l in range(DEPTH):
                layer(l)
            l = DEPTH
            dve.wait_ge(*at("ssq_ready", l, 0))
            link(l, V.tensor_reduce(y_a[:, 0:2], ssq.rearrange("p (t j) -> p t j", j=4), AX.X, ALU.add))
            link(l, V.tensor_scalar(y_in[:, 0:2], y_a[:, 0:2], 1.0 / D_MODEL, EPS, ALU.mult, ALU.add))
            rsqrt(l, 2, r_norm)
            dve.wait_ge(fin_row_sem, 16)
            for t in range(NT):
                V.scalar_tensor_tensor(out=fin[:, t, :], in0=x_res[:, t, :], scalar=r_norm[:, t:t + 1], in1=fin_row,
                                       op0=ALU.mult, op1=ALU.mult).then_inc(fin_sem, 1)

        @block.gpsimd
        def _(pool):
            G = nc.gpsimd
            chain = Chain(pool, "gpsimd_done", 0)

            def rope(l, buf, tb, heads, half, sin, n, units_):
                for u in units_:
                    wait_pair_freed(pool, l, u)
                w = heads * 2 * half
                for t in range(NT):
                    s = cst(sin, NT)[:, t, :].unsqueeze(1).unsqueeze(1).to_broadcast([P, heads, 2, half])
                    signal(G.tensor_tensor(tb[:, t, 0:w].rearrange("p (h a d) -> p h a d", a=2, d=half),
                                           buf[:, t, 0:w].rearrange("p (h a d) -> p h a d", a=2, d=half), s, ALU.mult),
                           "rope_b")

            def triangle_rows(l, g):
                if g == 0:
                    wait_freed(pool, l, ("aoT", 1, 1))
                    pool.wait_ge(*at("gate_g", l, 1))
                else:
                    wait_full(pool, l, ("o1", g - 1))
                for t in range(NT):
                    for h in range(GH):
                        c = ci(t, g, h)
                        ins = G.tensor_scalar(trig[:, t * GH + h, :], cst("tri"), gate[:, c:c + 1], None, ALU.mult)
                        if t * GH + h < NC - 1:
                            chain.run(ins)
                chain.settle(l)
                signal(ins, "trig_ready")

            def off_diagonals(l, g):
                for lev in range(LEVELS):
                    if lev == 0:
                        for t in range(NT):
                            wait_freed(pool, l, ("kk", g, t))
                    else:
                        wait_full(pool, l, ("R", g, lev - 1, 1))
                        if lev == 1:
                            pool.wait_ge(*at("t_ready", l, g + 1))
                    signal(G.tensor_tensor(aoff, amat, each(level[:, lev, :], NC), ALU.mult), "off_ready")

            for l in range(DEPTH):
                pool.wait_ge(*at("rows_landed", l, 48))
                signal(G.affine_select(out=sgw[:], in_=sgw[:], compare_op=ALU.is_ge, fill=0.0, base=0,
                                       pattern=[[0, SG_GROUPS], [-1, P]], channel_multiplier=1), "gate_w")
                for t in range(NT):
                    pool.wait_ge(*at("gate_norm", l, t + 1))
                    chain.link(l, G.tensor_tensor(zv[:, t, :], zv[:, t, :], ln_rows[:, 0, :], ALU.mult))
                    signal(G.tensor_tensor(zv[:, t, :], zv[:, t, :], ln_rows[:, 1, :], ALU.add), "gate_v")
                rope(l, ibuf, tmp_b, IDX_HEADS + 1, 32, "sin_i", 0, [U["I0"], U["I1"], U["I2"]])
                rope(l, cbuf, rope_b, SA_HEADS + 1, 64, "sin_h", 2, [U["C0"], U["C1"]])
                for t in range(NT):
                    pool.wait_ge(*at("score_done", l, t + 1))
                    w = work[:, t, 0:(t + 1) * P]
                    signal(G.affine_select(out=w, in_=w, compare_op=ALU.is_ge, fill=NEG, base=t * P,
                                           pattern=[[-1, (t + 1) * P]], channel_multiplier=1), "masked")
                pool.wait_ge(*at("topk_done", l, 1))
                m = mbias[:, 0, 0:P]
                signal(G.affine_select(out=m, in_=m, compare_op=ALU.is_ge, fill=-OFF, base=0, pattern=[[-1, P]],
                                       channel_multiplier=1), "mask_ready")
                triangle_rows(l, 0)
                off_diagonals(l, 0)
                triangle_rows(l, 1)
                off_diagonals(l, 1)
                for n in range(16):
                    q, j = n // 4, n % 4
                    wait_pair_freed(pool, l, U[f"U{q}{j}"])
                    if n >= 2:
                        wait_full(pool, l, ("hT", (n - 2) // 4, (n - 2) % 4, 1))
                    signal(G.tensor_tensor(h_sq[:, j % 2, :], h_relu[:, j % 2, :], h_relu[:, j % 2, :], ALU.mult),
                           "h_sq_ready")

        for name, n in counts.items():
            unit = 16 if name.endswith("landed") else 1
            if unit == 1:
                extra = 8 if name == "ssq_ready" else 0
                assert n == PER_LAYER[name] * DEPTH + extra, (name, n)


_INS = ["x", "mem", "ln_mix", "w_in", "conv_w", "a_log", "dt_bias", "gdn_norm", "sg_ln_g", "sg_ln_b", "sg_w", "sg_b",
        "w_out", "ln_cross", "ln_mem", "w_q_mem", "w_kv_mem", "w_o_mem", "ln_mlp", "w_up", "w_down", "ln_final"]


def kernel(**inputs):
    import concourse.bacc as bacc
    from concourse.bass_utils import run_bass_kernel_spmd

    nc = bacc.Bacc("TRN2", target_bir_lowering=False, num_devices=1)
    arrays = {"consts": shape_constants()}
    args = [nc.dram_tensor("consts", (P, N_CONST), F32, kind="ExternalInput").ap()]
    for name in _INS:
        a = np.ascontiguousarray(inputs[name])
        arrays[name + "_dram"] = a
        args.append(nc.dram_tensor(name + "_dram", a.shape, mybir.dt.from_np(a.dtype), kind="ExternalInput").ap())
    args.append(nc.dram_tensor("out_dram", (1, SEQ, D_MODEL), F32, kind="ExternalOutput").ap())
    trunk(nc, *args)
    r = run_bass_kernel_spmd(nc, [arrays], core_ids=[0])
    return r.results[0]["out_dram"]
```

```python
from contextlib import ExitStack

import numpy as np

import concourse.bass as bass
from concourse import mybir

F32 = mybir.dt.float32
F32R = mybir.dt.float32r
I32 = mybir.dt.int32
ALU = mybir.AluOpType
ACT = mybir.ActivationFunctionType
AX = mybir.AxisListType

P = 128
D_MODEL, SEQ, DEPTH, MEM_LEN = 2048, 256, 2, 256
NT = SEQ // P
KT = D_MODEL // P
HEAD = 128
GDN_HEADS, SG_GROUPS, SA_HEADS, IDX_HEADS, IDX_DIM, MEM_HEADS = 6, 4, 6, 16, 64, 4
CONV_K, TOPK, EPS = 4, SEQ // 4, 1e-6
D_A, D_B, D_C, D_MEM, D_FF = GDN_HEADS * HEAD, SG_GROUPS * HEAD, SA_HEADS * HEAD, MEM_HEADS * HEAD, 4 * D_MODEL
GH = GDN_HEADS // 2
NC = GH * NT
LEVELS = 7
COL = 512
RING = 4
NEG, TAKEN, OFF = -1e38, -3e38, 1e30
SCALE = HEAD ** -0.5

C_QKV, C_Z, C_DEC = 0, 3 * D_A, 4 * D_A
C_BU = C_DEC + 2 * GDN_HEADS
C_BV, C_Q = C_BU + D_B, C_BU + 2 * D_B
C_IQ = C_Q + D_C + 2 * HEAD
C_IK = C_IQ + IDX_HEADS * IDX_DIM
D_IN = C_IK + IDX_DIM + IDX_HEADS
ZREST = C_BU - (C_Z + COL)
IREST = D_IN - C_IK
IW = IDX_HEADS * IDX_DIM + IREST

CONST = {}
_at = 0
for _name, _w in (("ident", P), ("tri", P), ("strict", P), ("incl", P), ("ones", P), ("level", LEVELS * P),
                  ("cos_h", NT * 64), ("sin_h", NT * 64), ("cos_i", NT * 32), ("sin_i", NT * 32)):
    CONST[_name] = (_at, _at + _w)
    _at += _w
N_CONST = _at


def shape_constants():
    c = np.zeros((P, N_CONST), np.float32)
    p, f = np.arange(P)[:, None], np.arange(P)[None, :]

    def put(name, a):
        c[:, CONST[name][0]:CONST[name][1]] = a

    put("ident", p == f)
    put("tri", p <= f)
    put("strict", np.where(f < p, 0, OFF))
    put("incl", np.where(f >= p, 0, OFF))
    put("ones", 1)
    lev = [((p >> b) % 2 == 1) & ((f >> b) == (p >> b) - 1) for b in range(LEVELS)]
    put("level", np.concatenate(lev, 1))
    for name, dim in (("h", HEAD), ("i", IDX_DIM)):
        inv = np.float32(10000.0) ** (-np.arange(0, dim, 2, dtype=np.float32) / np.float32(dim))
        ang = np.arange(SEQ, dtype=np.float32)[:, None] * inv.astype(np.float32)[None, :]
        for fn, what in ((np.cos, "cos_"), (np.sin, "sin_")):
            put(what + name, fn(ang).astype(np.float32).reshape(NT, P, dim // 2).transpose(1, 0, 2).reshape(P, -1))
    return c


class Unit:

    def __init__(self, name, mat, r0, tiles, c0, width, form, act, first_tile):
        self.first_tile = first_tile
        self.name, self.mat, self.r0, self.tiles, self.c0 = name, mat, r0, tiles, c0
        self.width, self.form, self.act = width, form, act
        self.pieces = tiles // 2

    def tile(self, p, i):
        return (self.first_tile + 2 * p + i) % self.tiles


def layer_units():
    u = []

    def add(name, mat, c0, width, form="tok", act="A", r0=0, tiles=KT, first_tile=0):
        u.append(Unit(name, mat, r0, tiles, c0, width, form, act, first_tile))

    add("B1", "w_in", C_BV, D_B)
    add("B0", "w_in", C_BU, D_B)
    for j in range(3):
        add(f"I{j}", "w_in", C_IQ + j * IW // 3, IW // 3)
    add("C0", "w_in", C_Q, COL)
    add("C1", "w_in", C_Q + COL, COL)
    for g in range(2):
        for s in range(3):
            if g == 0 and s == 2:
                add("Z1", "w_in", C_Z + COL, ZREST)
            if g == 1 and s == 2:
                add("Z0", "w_in", C_Z, COL)
            add(f"{'QKV'[s]}{g}", "w_in", C_QKV + s * D_A + g * GH * HEAD, GH * HEAD, "ch")
    add("KM", "w_kv_mem", 0, D_MEM, "ch")
    add("VM", "w_kv_mem", D_MEM, D_MEM)
    for j in range(4):
        add(f"O{j}", "w_out", j * COL, COL, act="B", first_tile=GDN_HEADS)
    add("QM", "w_q_mem", 0, D_MEM, "ch")
    for j in range(4):
        add(f"OM{j}", "w_o_mem", j * COL, COL, act="B", tiles=MEM_HEADS)
    for q in range(4):
        for j in range(4):
            add(f"U{q}{j}", "w_up", q * D_MODEL + j * COL, COL)
        for j in range(4):
            add(f"D{q}{j}", "w_down", j * COL, COL, act="B", r0=q * D_MODEL)
    at = 0
    for n, x in enumerate(u):
        x.n, x.first = n, at
        at += x.pieces
    return u, at


def trunk(nc, consts, x, mem, ln_mix, w_in, conv_w, a_log, dt_bias, gdn_norm, sg_ln_g, sg_ln_b, sg_w, sg_b,
          w_out, ln_cross, ln_mem, w_q_mem, w_kv_mem, w_o_mem, ln_mlp, w_up, w_down, ln_final, out):
    units, PIECES = layer_units()
    U = {u.name: u for u in units}
    matrices = dict(w_in=w_in, w_out=w_out, w_q_mem=w_q_mem, w_kv_mem=w_kv_mem, w_o_mem=w_o_mem, w_up=w_up,
                    w_down=w_down)
    assert PIECES % RING == 0 and len(units) % 2 == 0

    with ExitStack() as ctx:
        def sb(name, shape, dt=F32):
            return ctx.enter_context(nc.sbuf_tensor(name, shape, dt))

        def sem(name):
            return ctx.enter_context(nc.semaphore(name))

        x_res = sb("x_res", [P, NT, D_MODEL])
        act = {a: (sb(f"act{a}_hi", [P, KT, SEQ], F32R), sb(f"act{a}_lo", [P, KT, SEQ], F32R)) for a in "AB"}
        w_raw = sb("w_raw", [P, RING, 2, COL])
        w_hi = sb("w_hi", [P, RING, 2, COL], F32R)
        w_lo = sb("w_lo", [P, RING, 2, COL], F32R)
        const = sb("const", [P, N_CONST])
        par_rows = sb("par_rows", [P, 2, P])
        par = sb("par", [P, 2, P])
        ln_rows = sb("ln_rows", [P, 2, D_B])
        sgw = sb("sgw", [P, SG_GROUPS, P])
        sgw_t = sb("sgw_t", [P, SG_GROUPS, P])
        small = sb("small", [P, 544])
        scratch = sb("scratch", [P, 15360])
        psum = ctx.enter_context(nc.psum_tensor("psum", [P, 8, COL], F32))

        def cst(name, n=None):
            a = const[:, CONST[name][0]:CONST[name][1]]
            return a.rearrange("p (t n) -> p t n", t=n) if n else a

        ident, ones = cst("ident"), cst("ones")
        level = cst("level", LEVELS)

        def region(start, *shape):
            n = int(np.prod(shape))
            a = scratch[:, start:start + n]
            if len(shape) == 2:
                a = a.rearrange("p (a b) -> p a b", b=shape[1])
            if len(shape) == 3:
                a = a.rearrange("p (a b c) -> p a b c", b=shape[1], c=shape[2])
            return a

        junk = region(0, NT, COL)
        mix_rows = region(8192, P)
        q_t = [region((1 - g) * 768, GH, SEQ) for g in range(2)]
        k_t, v_t = region(1536, GH, SEQ), region(2304, GH, SEQ)
        x_pad = region(3072, GH, SEQ + CONV_K - 1)
        kn, kn_t, vb, dec, dec_t, amat, aoff, rmat, umat, tmat = [region(3856 + 768 * i, NC, P) for i in range(10)]
        s1, w1 = region(11536, GH, P), region(11920, GH, P)
        qs = region(12304, GH, P)
        zz = region(12688, NT, D_A)
        vn, obuf, ksc = aoff, vb, tmat
        trig, sqq, sqk = aoff, dec, kn_t
        ibuf, cbuf = region(3856, NT, IW), region(6064, NT, 1024)
        tmp_a, tmp_b = region(8112, NT, 1104), region(10320, NT, 1104)
        iq_t, p_t = region(8112, NT, 8, P), region(8112, SA_HEADS, NT, P)
        cq_t, ck_t, ik_t = region(10320, SA_HEADS, SEQ), region(11856, SEQ), region(12112, SEQ)
        ik2 = region(12528, NT, P)
        rope_a, rope_b = region(0, NT, 896), region(1792, NT, 896)
        relu = region(12784, 2, COL)
        score, work, mbias = region(13808, NT, SEQ), region(14320, NT, SEQ), region(14832, NT, SEQ)
        logit = region(3856, SA_HEADS, SEQ)
        zu, zv, sq_junk = region(12784, NT, D_B), region(13808, NT, D_B), region(10320, NT, D_B)
        mem_x = region(4096, NT, D_MODEL)
        mem_c = [region(at, NT, COL) for at in (14224, 768)]
        diag, r_row = sgw[:, 0:NT, :], sgw[:, NT:2 * NT, :].rearrange("p a b -> p (a b)")
        qm_t, km_t, vm = region(8192, MEM_HEADS, SEQ), region(14224, MEM_HEADS, MEM_LEN), region(1536, NT, D_MEM)
        xlogit, xp_t = region(11264, NT, MEM_HEADS, MEM_LEN), region(13312, MEM_HEADS, NT, SEQ)
        h_relu, h_sq = region(4096, 2, 1024), region(6144, 2, 1024)
        fin_row, fin = region(4096, D_MODEL), region(8192, NT, D_MODEL)

        _sm = [0]

        def tiny(n):
            _sm[0] += n
            assert _sm[0] <= 544
            return small[:, _sm[0] - n:_sm[0]]

        ssq, ssq_mem, r_mem = tiny(8), tiny(2), tiny(2)
        y_in, y_a, y_b, y_r = tiny(16), tiny(16), tiny(16), tiny(16)
        r_norms = [tiny(2) for _ in range(3)]
        r_out, r_qk, r_o = tiny(2), [tiny(12) for _ in range(2)], tiny(NC)
        al, dtb = tiny(GDN_HEADS), tiny(GDN_HEADS)
        db = tiny(NT * 12)
        t_abs, t_ln, gate, beta, eal = tiny(12), tiny(12), tiny(12), tiny(12), tiny(6)
        gcum, ngcum, eg, beg = tiny(12), tiny(12), tiny(12), tiny(12)
        glast, egl = tiny(GH), tiny(GH)
        mean, rstd, mcol = tiny(2), tiny(2), tiny(4)
        iw = tiny(NT * IDX_HEADS)
        max8 = tiny(2 * 8)
        mix_gain = tiny(DEPTH * KT)
        smax, ssum, sinv = tiny(12), tiny(12), tiny(12)
        xmax, xsum, xinv = tiny(8), tiny(8), tiny(8)
        o_c, o_f = tiny(NC), tiny(NC)
        act_junk = tiny(1)

        PAR_ROWS = (3 * KT + SG_GROUPS + 1, CONV_K * 3 * GDN_HEADS)
        PAR = dict(ln_cross=(0, 0), ln_mem=(0, 16), ln_mlp=(0, 32), sg_b=(0, 48), gdn=(0, 52))
        NORM_GAIN = {1: "ln_cross", 2: "ln_mlp", 3: "ln_mem"}

        def gain(name, i):
            row, at = PAR[name]
            return par[:, row, at + i:at + i + 1]

        def conv_tap(j, ct):
            return par[:, 1, j * 18 + ct:j * 18 + ct + 1]

        w_landed = [sem(f"w_landed{i}") for i in range(RING)]
        hi_ready, lo_ready = sem("hi_ready"), sem("lo_ready")
        piece_done = sem("piece_done")
        pair_free = [sem(f"pair_free{i}") for i in range(2)]
        bank_full = [sem(f"bank_full{i}") for i in range(4)]
        bank_free = [sem(f"bank_free{i}") for i in range(4)]
        PER_LAYER = {}
        counts = {}
        sems = {}

        def declare(**kw):
            for name, n in kw.items():
                PER_LAYER[name] = n
                sems[name] = sem(name)
                counts[name] = 0

        BASE = dict(ssq_ready=8, act_hi=12)

        def at(name, l, i):
            assert 0 <= i <= PER_LAYER[name], (name, i)
            return sems[name], BASE.get(name, 0) + l * PER_LAYER[name] + i

        def signal(ins, name):
            counts[name] += 1
            return ins.then_inc(sems[name], 1)

        declare(
            params_landed=8 * 16, rows_landed=3 * 16,
            ssq_ready=24,
            r_ready=3, diag_ready=2,
            act_hi=64, gdn_hi=6, gate_hi=4, att_hi=4, xat_hi=4, ffn_hi=32,
            mem_scaled=4,
            gate_nmean=1, gate_var=2, gate_norm=2, gate_v=2, gate_w=1,
            rope_b=4, rope_done=5, relu_used=12, score_done=2, masked=2, topk_done=2, mask_ready=1,
            logits_ready=2, att_exp=12, att_p=2,
            conv_out=6, silu_out=6, sqs=4,
            db_ready=1, abs_ready=1, beta_exp=1, dec_ln=1, eal_ready=1, gate_g=1, beta_ready=1,
            eg_ready=1, beg_ready=1, trig_ready=2, kd_arg=2, egl_ready=2, dec_val=4, off_ready=14, t_ready=2,
            ksc_ready=4, o_ready=2,
            xlog_ready=2, xexp=4, xp_ready=2,
            h_sq_ready=16,
        )
        fin_sem, out_sem, mem_sem = sem("final_scaled"), sem("out_landed"), sem("mem_all_landed")
        const_sem, const_rest_sem, mem_squared = sem("ident_landed"), sem("consts_landed"), sem("mem_squared")
        x_sem = [sem(f"x_landed{i}") for i in range(4)]
        r_mem_ready, mix_landed = sem("r_mem_ready"), sem("ln_mix_landed")
        mix_turned, mix_ready = sem("ln_mix_turned"), sem("ln_mix_ready")
        mem_landed = [sem(f"mem_landed{i}") for i in range(2)]
        fin_row_sem = sem("fin_row_landed")

        class Chain:

            def __init__(self, eng, name, per_layer):
                self.eng, self.sem, self.per, self.k, self.base = eng, sem(name), per_layer, 0, 0

            def run(self, ins):
                self.k += 1
                ins.then_inc(self.sem, 1)

            def settle(self, l):
                self.eng.wait_ge(self.sem, self.base + l * self.per + self.k)

            def link(self, l, ins):
                self.run(ins)
                self.settle(l)

            def end_layer(self):
                assert self.k == self.per, (self.sem, self.k)
                self.k = 0

        def wait(eng, s, v):
            if not (isinstance(v, int) and v <= 0):
                eng.wait_ge(s, v)

        uses, piece_before = {}, {}
        USES = 276
        BPL = USES // 4
        NEXT = [("norm", 0, kt) for kt in range(12)]
        for name in NEXT:
            uses[name] = USES - len(NEXT) + name[2]

        def norm_use(l, w, kt):
            if w == 0:
                g = mix_gain[:, l * KT + kt:l * KT + kt + 1]
                return (("norm", 0, kt), l - 1, 52 + kt + 1, g) if kt < 12 else (("norm", 0, kt), l, kt - 12 + 1, g)
            name = ("mem", kt) if w == 3 else ("norm", w, kt)
            return name, l, {3: 4, 1: 20, 2: 36}[w] + kt + 1, gain(NORM_GAIN[w], kt)

        def bank_of(name):
            n = uses[name]
            return psum[:, 4 + n % 4, :]

        def wait_full(eng, l, name):
            n = uses[name]
            eng.wait_ge(bank_full[n % 4], 3 + l * BPL + n // 4 + 1)

        def free(ins, name):
            ins.then_inc(bank_free[uses[name] % 4], 1)

        def wait_freed(eng, l, name):
            n = uses[name]
            eng.wait_ge(bank_free[n % 4], 3 + l * BPL + n // 4 + 1)

        def score_head(n, i, per):
            return 2 * (n // 2 * per + i) + n % 2

        def half(a, lev, bit):
            flat = a.rearrange("p h n -> p (h n)")
            return flat.rearrange("p (x two w) -> p x two w", two=2, w=1 << lev)[:, :, bit, :]

        def packed(b, lev, blocks):
            return b[:, 0:blocks * P // 2].rearrange("p (x w) -> p x w", w=1 << lev)

        def pair(u):
            i = 2 * (u.n % 2)
            return psum[:, i:i + 2, :]

        def pair_ch(u):
            return pair(u).rearrange("p a (c t) -> p (a c) t", t=SEQ)

        def wait_unit(eng, l, u):
            eng.wait_ge(piece_done, l * PIECES + u.first + u.pieces)

        def free_pair(ins, u):
            ins.then_inc(pair_free[u.n % 2], 1)

        def wait_pair_freed(eng, l, u):
            eng.wait_ge(pair_free[u.n % 2], l * (len(units) // 2) + u.n // 2 + 1)

        CONV = {f"{'QKV'[s]}{g}": (s, g) for g in range(2) for s in range(3)}
        SILU_LATE = 4

        block = ctx.enter_context(nc.Block())

        @block.tensor
        def _(pe):
            tp = nc.tensor.transpose

            def mm(o, a, b, start=True, stop=True, **kw):
                return nc.tensor.matmul(o, a, b, start=start, stop=stop, **kw)

            cnt, last_piece = [0], [-1]

            def take(l, name):
                n = cnt[0]
                cnt[0] += 1
                assert uses.get(name, n) == n, (name, n)
                uses[name] = n
                piece_before[name] = last_piece[0]
                wait(pe, bank_free[n % 4], 3 + l * BPL + n // 4)
                return psum[:, 4 + n % 4, :]

            def full(ins, name):
                ins.then_inc(bank_full[uses[name] % 4], 1)

            def gemm(l, u, p0=0, p1=None, needs=None):
                hi, lo = act[u.act]
                if p0 == 0:
                    wait(pe, pair_free[u.n % 2], l * (len(units) // 2) + u.n // 2)
                for p in range(p0, u.pieces if p1 is None else p1):
                    g = u.first + p
                    s = g % RING
                    pe.wait_ge(lo_ready, l * PIECES + g + 1)
                    for i in range(2):
                        kt = u.tile(p, i)
                        for name in (needs(kt) if needs else ()):
                            wait_freed(pe, l - (name in NEXT), name)
                        a, z = 2 * p + i == 0, 2 * p + i == u.tiles - 1
                        if u.form == "tok":
                            for t in range(NT):
                                o, tt = pair(u)[:, t, 0:u.width], slice(t * P, t * P + P)
                                wh, wl = w_hi[:, s, i, 0:u.width], w_lo[:, s, i, 0:u.width]
                                mm(o, hi[:, kt, tt], wh, start=a, stop=False)
                                mm(o, hi[:, kt, tt], wl, start=False, stop=False)
                                last = mm(o, lo[:, kt, tt], wh, start=False, stop=z)
                        else:
                            for c in range(u.width // P):
                                o, cc = pair_ch(u)[:, c, :], slice(c * P, c * P + P)
                                mm(o, w_hi[:, s, i, cc], hi[:, kt, :], start=a and c % 2 == 0, stop=False,
                                   skip_group_check=True)
                                mm(o, w_hi[:, s, i, cc], lo[:, kt, :], start=False, stop=False,
                                   skip_group_check=True)
                                last = mm(o, w_lo[:, s, i, cc], hi[:, kt, :], start=False, stop=z,
                                          skip_group_check=True)
                    last.then_inc(piece_done, 1)
                    last_piece[0] = g

            def norm_tile(l, w, kt):
                b = take(l, ("norm", w, kt))
                for t in range(NT):
                    last = tp(b[:, t * P:t * P + P], x_res[:, t, kt * P:kt * P + P], ident)
                full(last, ("norm", w, kt))

            def norm_chunk(l, w, j, u, at_l):
                if at_l >= 0:
                    wait_pair_freed(pe, at_l, u)
                for kt in range(4 * j, 4 * j + 4):
                    norm_tile(l, w, kt)

            def r_on_rows(l, w):
                pe.wait_ge(*at("diag_ready", l, w + 1))
                for t in range(NT):
                    b = take(l, ("row", w, t))
                    full(mm(b[:, 0:P], ones, diag[:, t, :]), ("row", w, t))

            def needed(u):
                w = dict(B1=0, KM=3, QM=1, U00=2).get(u.name)
                if w is None:
                    return None
                return lambda kt: [("mem", kt) if w == 3 else ("norm", w, kt)]

            stream = [(u, p) for u in units if u.n <= U["VM"].n for p in range(u.pieces)]
            pos = [0]

            def fill(l, n=None, to=None):
                while pos[0] < len(stream) and (n is None or n > 0):
                    u, p = stream[pos[0]]
                    if to is not None and u.n > U[to].n:
                        return
                    gemm(l, u, p, p + 1, needs=needed(u))
                    pos[0] += 1
                    if n is not None and not (u.name in CONV and p == u.pieces - 1):
                        n -= 1

            def turned(l, g, name, src):
                for t in range(NT):
                    b = take(l, (name, g, t))
                    for h in range(GH):
                        last = tp(b[:, h * P:h * P + P], src[:, h, t * P:t * P + P], ident)
                    full(last, (name, g, t))

            def gdn_sums(l, g):
                combos = [(t, h) for t in range(NT) for h in range(GH)]
                assert last_piece[0] >= U[f"Q{g}"].first + 15 + SILU_LATE, last_piece
                pe.wait_ge(*at("sqs", l, 2 * g + 2))
                b = take(l, ("ssq", g))
                for s, sq in enumerate((sqq, sqk)):
                    sqv = sq.rearrange("p (h t) n -> p h (t n)", h=GH)
                    for t, h in combos:
                        c = s * NC + t * GH + h
                        last = mm(b[:, c:c + 1], sqv[:, h, t * P:t * P + P], ones[:, 0:1])
                full(last, ("ssq", g))

            def turned_v(l, g):
                assert last_piece[0] >= U[f"V{g}"].first + 7 + SILU_LATE, last_piece
                pe.wait_ge(*at("silu_out", l, 3 * g + 3))
                turned(l, g, "v", v_t)

            def gdn_group(l, g, gaps):
                fill(l, gaps[0])
                turned(l, g, "k", k_t)
                fill(l, gaps[6])
                for t in range(NT):
                    wait_freed(pe, l, ("k", g, t))
                    b = take(l, ("kn", g, t))
                    for h in range(GH):
                        last = tp(b[:, h * P:h * P + P], kn[:, t * GH + h, :], ident)
                    full(last, ("kn", g, t))
                fill(l, gaps[7])
                if g == 0:
                    pe.wait_ge(*at("gate_g", l, 1))
                    b = take(l, "gcum")
                    full(mm(b[:, 0:12], cst("tri"), gate), "gcum")
                pe.wait_ge(*at("trig_ready", l, g + 1))
                for t in range(NT):
                    b = take(l, ("grow", g, t))
                    full(mm(b[:, 0:GH * P], ones, trig[:, t * GH:t * GH + GH, :]), ("grow", g, t))
                fill(l, gaps[1])
                fill(l, gaps[2])
                for t in range(NT):
                    wait_freed(pe, l, ("kn", g, t))
                    b = take(l, ("kk", g, t))
                    for h in range(GH):
                        i = t * GH + h
                        last = mm(b[:, h * P:h * P + P], kn_t[:, i, :], kn_t[:, i, :])
                    full(last, ("kk", g, t))
                for t in range(NT):
                    b = take(l, ("kq", g, t))
                    for h in range(GH):
                        last = mm(b[:, h * P:h * P + P], kn_t[:, t * GH + h, :], q_t[g][:, h, t * P:t * P + P])
                    full(last, ("kq", g, t))
                fill(l, gaps[3])
                if g == 1:
                    mem_chunk(l, 0)
                for lev in range(LEVELS):
                    if lev:
                        fill(l, gaps[4])
                    if lev == 3 and g == 0:
                        fill(l, to="V0")
                        turned_v(l, g)
                    if lev == 5 and g == 1:
                        turned_v(l, g)
                    if lev == 3 and g == 1:
                        gdn_out(l, 0)
                    pe.wait_ge(*at("off_ready", l, g * LEVELS + lev + 1))
                    for t in range(NT):
                        if lev:
                            wait_freed(pe, l, ("U", g, lev - 1, t))
                        b = take(l, ("R", g, lev, t))
                        for h in range(GH):
                            i = t * GH + h
                            if lev == LEVELS - 1:
                                last = mm(b[:, h * P // 2:(h + 1) * P // 2], aoff[:, i, :], umat[:, i, P // 2:])
                            else:
                                last = mm(b[:, h * P:h * P + P], aoff[:, i, :], umat[:, i, :] if lev else ident)
                        full(last, ("R", g, lev, t))
                    if lev == 0:
                        for t in range(NT):
                            uses[("U", g, 0, t)] = uses[("R", g, 0, t)]
                            piece_before[("U", g, 0, t)] = last_piece[0]
                        fill(l, 1)
                        continue
                    if g == 1 and lev < 4:
                        mem_chunk(l, lev)
                    fill(l, gaps[5])
                    for t in range(NT):
                        wait_freed(pe, l, ("R", g, lev, t))
                        if lev == 1:
                            pe.wait_ge(*at("t_ready", l, g + 1))
                        else:
                            wait_freed(pe, l, ("T", g, lev - 1, t))
                        b = take(l, ("U", g, lev, t))
                        for h in range(GH):
                            i = t * GH + h
                            last = mm(packed(b[:, h * P // 2:], lev, 1), tmat[:, i, :], half(rmat[:, i:i + 1, :], lev, 1))
                        full(last, ("U", g, lev, t))
                        if lev < LEVELS - 1:
                            b = take(l, ("T", g, lev, t))
                            for h in range(GH):
                                i = t * GH + h
                                last = mm(packed(b[:, h * P // 2:], lev, 1), rmat[:, i, :],
                                          half(tmat[:, i:i + 1, :], lev, 0))
                            full(last, ("T", g, lev, t))

            def gdn_scan(l, g, gaps):
                fill(l, gaps[0])
                wait_freed(pe, l, ("v", g, 0))
                wait_freed(pe, l, ("U", g, LEVELS - 1, 0))
                b = take(l, ("vn0", g))
                for h in range(GH):
                    last = mm(b[:, h * P:h * P + P], umat[:, h, :], vb[:, h, :])
                full(last, ("vn0", g))
                wait_freed(pe, l, ("v", g, 1))
                wait_freed(pe, l, ("U", g, LEVELS - 1, 1))
                pe.wait_ge(*at("ksc_ready", l, 2 * g + 2))
                b = take(l, ("w1", g))
                for h in range(GH):
                    last = mm(b[:, h * P:h * P + P], ksc[:, GH + h, :], umat[:, GH + h, :])
                full(last, ("w1", g))
                fill(l, gaps[1])
                wait_freed(pe, l, ("vn0", g))
                b = take(l, ("s1", g))
                for h in range(GH):
                    last = mm(b[:, h * P:h * P + P], ksc[:, h, :], vn[:, h, :])
                full(last, ("s1", g))
                for t in range(NT):
                    wait_freed(pe, l, ("kq", g, t))
                b = take(l, ("o0", g))
                for h in range(GH):
                    last = mm(b[:, h * P:h * P + P], dec_t[:, h, :], vn[:, h, :])
                full(last, ("o0", g))
                fill(l, gaps[2])
                wait_freed(pe, l, ("w1", g))
                wait_freed(pe, l, ("s1", g))
                b = take(l, ("vn1", g))
                for h in range(GH):
                    mm(b[:, h * P:h * P + P], umat[:, GH + h, :], vb[:, GH + h, :], stop=False)
                    last = mm(b[:, h * P:h * P + P], w1[:, h, :], s1[:, h, :], start=False)
                full(last, ("vn1", g))
                b = take(l, ("qs", g))
                for h in range(GH):
                    last = mm(b[:, h * P:h * P + P], q_t[g][:, h, P:2 * P], s1[:, h, :])
                full(last, ("qs", g))
                fill(l, gaps[3])
                wait_freed(pe, l, ("vn1", g))
                b = take(l, ("o1", g))
                for h in range(GH):
                    last = mm(b[:, h * P:h * P + P], dec_t[:, GH + h, :], vn[:, GH + h, :])
                full(last, ("o1", g))

            def gdn_out(l, g):
                pe.wait_ge(*at("o_ready", l, g + 1))
                for h in range(GH):
                    b = take(l, ("oT", g, h))
                    for t in range(NT):
                        last = tp(b[:, t * P:t * P + P], obuf[:, t * GH + h, :], ident)
                    full(last, ("oT", g, h))

            def gate_weights(l):
                pe.wait_ge(*at("gate_w", l, 1))
                b = take(l, "sgw")
                for i in range(SG_GROUPS):
                    last = tp(b[:, i * P:i * P + P], sgw[:, i, :], ident)
                full(last, "sgw")

            def gate_mix(l):
                wait_freed(pe, l, "sgw")
                for t in range(NT):
                    pe.wait_ge(*at("gate_v", l, t + 1))
                    b = take(l, ("sg", t))
                    for i in range(SG_GROUPS):
                        last = mm(b[:, i * P:i * P + P], sgw_t[:, i, :], zv[:, t, i * P:i * P + P])
                    full(last, ("sg", t))

            def gate_out(l):
                for t in range(NT):
                    wait_freed(pe, l, ("sg", t))
                for i in range(SG_GROUPS):
                    b = take(l, ("bT", i))
                    for t in range(NT):
                        last = tp(b[:, t * P:t * P + P], zu[:, t, i * P:i * P + P], ident)
                    full(last, ("bT", i))

            def idx_transposes(l):
                pe.wait_ge(*at("rope_done", l, 3))
                b = take(l, "ikT")
                for t in range(NT):
                    last = tp(b[:, t * P:t * P + P], ik2[:, t, :], ident)
                full(last, "ikT")
                for t in range(NT):
                    for half in range(2):
                        b = take(l, ("iqT", t, half))
                        for i in range(4):
                            c = (half * 4 + i) * P
                            last = tp(b[:, i * P:i * P + P], ibuf[:, t, c:c + P], ident)
                        full(last, ("iqT", t, half))

            def idx_scores(l, t, gap):
                width = (t + 1) * P
                per = COL // width
                wait_freed(pe, l, "ikT")
                for half in range(2):
                    wait_freed(pe, l, ("iqT", t, half))
                for n in range(IDX_HEADS // per):
                    if n % 2 == 0:
                        fill(l, gap)
                    b = take(l, ("score", t, n))
                    for i in range(per):
                        h = score_head(n, i, per)
                        r = slice((h % 2) * 64, (h % 2) * 64 + 64)
                        last = mm(b[:, i * width:(i + 1) * width], iq_t[r, t, h // 2, :], ik_t[r, 0:width])
                    full(last, ("score", t, n))

            def att_transposes(l):
                pe.wait_ge(*at("rope_done", l, 5))
                b = take(l, "ckT")
                for t in range(NT):
                    last = tp(b[:, t * P:t * P + P], cbuf[:, t, D_C:D_C + P], ident)
                full(last, "ckT")
                for n in range(3):
                    b = take(l, ("cqT", n))
                    for i in range(2):
                        h = 2 * n + i
                        for t in range(NT):
                            c = i * SEQ + t * P
                            last = tp(b[:, c:c + P], cbuf[:, t, h * P:h * P + P], ident)
                    full(last, ("cqT", n))

            def att_logits(l, t):
                width = (t + 1) * P
                per = 3 if t == 0 else 2
                wait_freed(pe, l, "ckT")
                for n in range(3):
                    wait_freed(pe, l, ("cqT", n))
                for n in range(SA_HEADS // per):
                    b = take(l, ("logit", t, n))
                    for i in range(per):
                        h = n * per + i
                        last = mm(b[:, i * width:(i + 1) * width], cq_t[:, h, t * P:t * P + P], ck_t[:, 0:width])
                    full(last, ("logit", t, n))

            def att_out(l, t, gap):
                pe.wait_ge(*at("att_p", l, t + 1))
                for s in range(t + 1):
                    for n in range(2):
                        b = take(l, ("pT", t, s, n))
                        for i in range(GH):
                            last = tp(b[:, i * P:i * P + P], logit[:, n * GH + i, s * P:s * P + P], ident)
                        full(last, ("pT", t, s, n))
                fill(l, gap)
                for n in range(2):
                    for s in range(t + 1):
                        wait_freed(pe, l, ("pT", t, s, n))
                    b = take(l, ("aoT", t, n))
                    for i in range(GH):
                        for s in range(t + 1):
                            last = mm(b[:, i * P:i * P + P], cbuf[:, s, D_C + P:D_C + 2 * P],
                                      p_t[:, n * GH + i, s, :], start=s == 0, stop=s == t)
                    full(last, ("aoT", t, n))

            def mem_chunk(l, c):
                pe.wait_ge(*at("mem_scaled", l, c + 1))
                for kt in range(4 * c, 4 * c + 4):
                    b = take(l, ("mem", kt))
                    for t in range(NT):
                        o = (kt % 4) * P
                        last = tp(b[:, t * P:t * P + P], mem_c[c % 2][:, t, o:o + P], ident)
                    full(last, ("mem", kt))

            def cross_logits(l):
                wait_pair_freed(pe, l, U["KM"])
                wait_pair_freed(pe, l, U["QM"])
                for t in range(NT):
                    for n in range(2):
                        b = take(l, ("xlogit", t, n))
                        for i in range(2):
                            h = 2 * n + i
                            last = mm(b[:, i * SEQ:(i + 1) * SEQ], qm_t[:, h, t * P:t * P + P], km_t[:, h, :])
                        full(last, ("xlogit", t, n))

            def cross_out(l):
                for t in range(NT):
                    pe.wait_ge(*at("xp_ready", l, t + 1))
                    for s in range(NT):
                        b = take(l, ("xpT", t, s))
                        for h in range(MEM_HEADS):
                            last = tp(b[:, h * P:h * P + P], xlogit[:, t, h, s * P:s * P + P], ident)
                        full(last, ("xpT", t, s))
                wait_pair_freed(pe, l, U["VM"])
                for t in range(NT):
                    for s in range(NT):
                        wait_freed(pe, l, ("xpT", t, s))
                for h in range(MEM_HEADS):
                    b = take(l, ("xo", h))
                    for s in range(NT):
                        last = mm(b[:, 0:SEQ], vm[:, s, h * P:h * P + P], xp_t[:, h, s, :], start=s == 0, stop=s == 1)
                    full(last, ("xo", h))

            def hidden(l, q, j):
                pe.wait_ge(*at("h_sq_ready", l, q * 4 + j + 1))
                for half in range(2):
                    b = take(l, ("hT", q, j, half))
                    for i in range(2):
                        for t in range(NT):
                            c = t * COL + (2 * half + i) * P
                            o = (i * NT + t) * P
                            last = tp(b[:, o:o + P], h_sq[:, j % 2, c:c + P], ident)
                    full(last, ("hT", q, j, half))

            def layer(l):
                cnt[0] = 0
                if l:
                    last_piece[0], pos[0] = -1, 0
                    fill(l, 2)
                norm_chunk(l, 0, 3, U["D33"], l - 1)
                pe.wait_ge(*at("params_landed", l, 8 * 16))
                for i in range(2):
                    b = take(l, ("par", i))
                    n = PAR_ROWS[i]
                    full(tp(b[:, 0:n], par_rows[0:n, i, :], ident[0:n, 0:n]), ("par", i))
                fill(l, to="B1")
                gate_weights(l)
                fill(l, to="B0")
                if l == 0:
                    pe.wait_ge(const_rest_sem, 16)
                r_on_rows(l, 0)
                fill(l, to="I0")
                gate_mix(l)
                fill(l, 4)
                gate_out(l)
                fill(l, to="C0")
                idx_transposes(l)
                fill(l, 2)
                idx_scores(l, 0, 1)
                idx_scores(l, 1, 1)
                fill(l, to="C1")
                fill(l, 6)
                att_transposes(l)
                fill(l, 1)
                att_logits(l, 0)
                fill(l, to="Q0")
                fill(l, 4)
                att_out(l, 0, 1)
                fill(l, 1)
                att_logits(l, 1)
                fill(l, 4)
                att_out(l, 1, 1)
                fill(l, 3)
                gdn_sums(l, 0)
                gdn_group(l, 0, (0, 1, 1, 1, 1, 1, 1, 4))
                gdn_scan(l, 0, (2, 1, 1, 1))
                fill(l, to="K1")
                fill(l, 6)
                gdn_sums(l, 1)
                gdn_group(l, 1, (0, 1, 0, 2, 1, 1, 1, 0))
                gdn_scan(l, 1, (1, 1, 1, 1))
                fill(l)

                def mixed(kt):
                    if kt < 6:
                        return [("oT", kt // GH, kt % GH)]
                    if kt < 10:
                        return [("bT", kt - 6)]
                    return [("aoT", t, (kt - 10) // GH) for t in range(NT)]

                gemm(l, U["O0"], 0, 6, needs=mixed)
                gdn_out(l, 1)
                gemm(l, U["O0"], 6, needs=mixed)
                for j in range(1, 4):
                    gemm(l, U[f"O{j}"], 0, 2)
                    norm_chunk(l, 1, j - 1, U[f"O{j - 1}"], l)
                    gemm(l, U[f"O{j}"], 2)
                gemm(l, U["QM"], 0, 2, needs=needed(U["QM"]))
                norm_chunk(l, 1, 3, U["O3"], l)
                gemm(l, U["QM"], 2, needs=needed(U["QM"]))
                r_on_rows(l, 1)
                cross_logits(l)
                cross_out(l)
                gemm(l, U["OM0"], needs=lambda kt: [("xo", kt)])
                for j in range(1, 4):
                    gemm(l, U[f"OM{j}"])
                    norm_chunk(l, 2, j - 1, U[f"OM{j - 1}"], l)
                for q in range(4):
                    if q == 0:
                        gemm(l, U["U00"], 0, 2, needs=needed(U["U00"]))
                        norm_chunk(l, 2, 3, U["OM3"], l)
                        gemm(l, U["U00"], 2, needs=needed(U["U00"]))
                    else:
                        gemm(l, U[f"U{q}0"])
                    for j in range(1, 4):
                        gemm(l, U[f"U{q}{j}"], 0, 4)
                        hidden(l, q, j - 1)
                        gemm(l, U[f"U{q}{j}"], 4)
                    need = lambda kt, q=q: [("hT", q, kt // 4, (kt % 4) // 2)]
                    gemm(l, U[f"D{q}0"], 0, 4, needs=need)
                    hidden(l, q, 3)
                    gemm(l, U[f"D{q}0"], 4, needs=need)
                    for j in range(1, 4):
                        gemm(l, U[f"D{q}{j}"], 0, 2)
                        if q == 3 and l < DEPTH - 1:
                            norm_chunk(l, 0, j - 1, U[f"D3{j - 1}"], l)
                        gemm(l, U[f"D{q}{j}"], 2)
                assert cnt[0] == USES - len(NEXT) * (l == DEPTH - 1), cnt[0]

            pe.wait_ge(const_sem, 16)
            pe.wait_ge(mix_landed, 16)
            tp(psum[:, 3, 0:DEPTH * KT], mix_rows[0:DEPTH * KT, :], ident[0:DEPTH * KT, 0:DEPTH * KT]).then_inc(mix_turned, 1)
            for kt in range(12):
                if kt % 4 == 0:
                    pe.wait_ge(x_sem[kt // 4], 16)
                n = uses[("norm", 0, kt)]
                wait(pe, bank_free[n % 4], 3 - BPL + n // 4)
                b = bank_of(("norm", 0, kt))
                for t in range(NT):
                    last = tp(b[:, t * P:t * P + P], x_res[:, t, kt * P:kt * P + P], ident)
                full(last, ("norm", 0, kt))
                if kt == 3:
                    pe.wait_ge(mix_ready, 1)
                    fill(0, 2)
            pe.wait_ge(x_sem[3], 16)
            for l in range(DEPTH):
                layer(l)

        assert not any(n[0] == "pad" for n in uses), uses

        @block.sync
        def _(sp):
            def params(l):
                if l > 0:
                    sp.wait_ge(*at("gate_g", l - 1, 1))
                land = sems["params_landed"]
                for i, v in enumerate((ln_cross, ln_mem, ln_mlp)):
                    sp.dma_start(par_rows[16 * i:16 * i + 16, 0, :], v[l].rearrange("(k p) -> k p", p=P)).then_inc(land, 16)
                sp.dma_start(par_rows[48:52, 0, :], sg_b[l]).then_inc(land, 16)
                sp.dma_start(par_rows[52:53, 0, :], gdn_norm[l:l + 1, :]).then_inc(land, 16)
                sp.dma_start(par_rows[0:72, 1, :], conv_w[l].rearrange("j (c p) -> (j c) p", p=P)).then_inc(land, 16)
                sp.dma_start(al, a_log[l:l + 1, :].to_broadcast([P, GDN_HEADS])).then_inc(land, 16)
                sp.dma_start(dtb, dt_bias[l:l + 1, :].to_broadcast([P, GDN_HEADS])).then_inc(land, 16)

            def rows(l):
                if l > 0:
                    sp.wait_ge(*at("gate_v", l - 1, 2))
                    wait_pair_freed(sp, l - 1, U["QM"])
                rows_landed = sems["rows_landed"]
                sp.dma_start(ln_rows[:, 0, :], sg_ln_g[l:l + 1, :].to_broadcast([P, D_B])).then_inc(rows_landed, 16)
                sp.dma_start(ln_rows[:, 1, :], sg_ln_b[l:l + 1, :].to_broadcast([P, D_B])).then_inc(rows_landed, 16)
                sp.dma_start(sgw[:], sg_w[l].rearrange("g t s -> t g s")).then_inc(rows_landed, 16)

            def x_chunk(j):
                c = slice(j * COL, j * COL + COL)
                sp.dma_start(x_res[:, :, c], x[0, :, c].rearrange("(t p) n -> p t n", p=P)).then_inc(x_sem[j], 16)

            sp.dma_start(const[:, 0:P], consts[:, 0:P]).then_inc(const_sem, 16)
            sp.dma_start(mix_rows[0:DEPTH * KT, :], ln_mix.rearrange("l (k p) -> (l k) p", p=P)).then_inc(mix_landed, 16)
            x_chunk(0)

            def chunk_after(c):
                return ("k", 1, 1) if c == 1 else ("mem", 4 * c - 5)

            def mem_chunk(l, c):
                if c == 0:
                    sp.wait_ge(*at("att_p", l, 2))
                else:
                    wait_full(sp, l, chunk_after(c))
                d = slice(c * COL, c * COL + COL)
                sp.dma_start(mem_c[c % 2], mem[0, :, d].rearrange("(t p) n -> p t n", p=P)).then_inc(mem_landed[c % 2], 16)

            for l in range(DEPTH):
                if l:
                    params(l)
                for u in units:
                    if u.name == "B0":
                        rows(l)
                        if l == 0:
                            for t in range(NT):
                                sp.dma_start(mem_x[:, t, :], mem[0, t * P:t * P + P, :]).then_inc(mem_sem, 16)
                    for p in range(u.pieces):
                        g = u.first + p
                        for c in range(1, 4):
                            if g == piece_before[chunk_after(c)] + RING + 1:
                                mem_chunk(l, c)
                        if u.name == "Q1" and p == 0:
                            mem_chunk(l, 0)
                        wait(sp, lo_ready, l * PIECES + g + 1 - RING)
                        r = u.r0 + u.tile(p, 0) * P
                        src = matrices[u.mat][l, r:r + 2 * P, u.c0:u.c0 + u.width].rearrange("(k p) n -> p k n", p=P)
                        sp.dma_start(w_raw[:, g % RING, :, 0:u.width], src).then_inc(w_landed[g % RING], 16)
                        if l == 0 and g < 3:
                            x_chunk(g + 1)
                        if l == 0 and g == 3:
                            params(0)
                            sp.dma_start(const[:, P:], consts[:, P:]).then_inc(const_rest_sem, 16)
            sp.wait_ge(*at("h_sq_ready", DEPTH - 1, 16))
            sp.dma_start(fin_row, ln_final.rearrange("(a n) -> a n", a=1).to_broadcast([P, D_MODEL])).then_inc(fin_row_sem, 16)
            for t in range(NT):
                sp.wait_ge(fin_sem, t + 1)
                sp.dma_start(out[0, t * P:t * P + P, :], fin[:, t, :]).then_inc(out_sem, 16)
            sp.wait_ge(out_sem, 32)

        def each(a, n):
            return a.unsqueeze(1).to_broadcast([P, n, a.shape[-1]])

        def ci(t, g, h):
            return t * GDN_HEADS + g * GH + h

        def unit_of(g):
            return [v for v in units if v.first <= g % PIECES][-1]

        ends = {u.first + u.pieces - 1: u for u in units}
        @block.scalar
        def _(sc):
            act_fn = nc.scalar.activation
            chain = Chain(sc, "scalar_done", 0)
            nxt = [0]

            def ahead(l, piece):
                while nxt[0] <= piece + RING:
                    g = nxt[0]
                    nxt[0] += 1
                    if l * PIECES + g < DEPTH * PIECES:
                        s, w = g % RING, unit_of(g).width
                        sc.wait_ge(w_landed[s], 16 * ((l * PIECES + g) // RING + 1))
                        wait(sc, piece_done, l * PIECES + g + 1 - RING)
                        act_fn(w_hi[:, s, :, 0:w], w_raw[:, s, :, 0:w], ACT.Copy).then_inc(hi_ready, 1)
                    if g - RING in ends:
                        wait(sc, piece_done, l * PIECES + g + 1 - RING)
                        result(l, ends[g - RING])
                    u = ends.get(g - RING - SILU_LATE)
                    if u and u.name in CONV:
                        for s in {"K": (0, 1), "V": (2,), "Q": ()}[u.name[0]]:
                            silu(l, s, CONV[u.name][1])

            def reach(l, name):
                ahead(l, piece_before[name])
                wait_full(sc, l, name)
                return bank_of(name)

            def copy_out(l, name, dst, n, scale=1.0, split=None):
                b = reach(l, name)[:, 0:n]
                if split:
                    b = b.rearrange("p (a b) -> p a b", b=split)
                free(act_fn(dst, b, ACT.Copy, scale=scale), name)

            def hi_part(l, name, dst, sig, scale=None):
                b = reach(l, name)[:, 0:int(np.prod(dst.shape[1:]))]
                if len(dst.shape) == 3:
                    b = b.rearrange("p (a b) -> p a b", b=dst.shape[2])
                if scale is None:
                    signal(act_fn(dst, b, ACT.Copy), sig)
                else:
                    signal(act_fn(dst, b, ACT.Identity, scale=scale), sig)

            def squares(n, j):
                for t in range(NT):
                    c = slice(j * COL, j * COL + COL)
                    wait(sc, sems["ssq_ready"], n + 2 * j + t - 1)
                    signal(act_fn(junk[:, t, :], x_res[:, t, c], ACT.Square, accum_out=ssq[:, t * 4 + j:t * 4 + j + 1]),
                           "ssq_ready")

            def norm_hi(l, w, kts):
                for kt in kts:
                    name, at_l, n, g = norm_use(l, w, kt)
                    if at_l >= 0:
                        ahead(at_l, piece_before[name])
                    wait_full(sc, at_l, name)
                    signal(act_fn(act["A"][0][:, kt, :], bank_of(name)[:, 0:SEQ], ACT.Identity, scale=g), "act_hi")

            def scaled(l, u, w, dst, fn, width, t, **kw):
                return act_fn(dst, pair(u)[:, t, 0:width], fn, scale=r_norms[w][:, t:t + 1], **kw)

            def result(l, u):
                name = u.name
                if name == "B1":
                    sc.wait_ge(*at("r_ready", l, 1))
                    for t in range(NT):
                        ins = scaled(l, u, 0, zv[:, t, :], ACT.Gelu_apprx_tanh, D_B, t, accum_out=mean[:, t:t + 1])
                    free_pair(ins, u)
                    sc.wait_ge(*at("gate_nmean", l, 1))
                    for t in range(NT):
                        signal(act_fn(sq_junk[:, t, :], zv[:, t, :], ACT.Square, bias=mean[:, t:t + 1],
                                      accum_out=rstd[:, t:t + 1]), "gate_var")
                elif name == "B0":
                    for t in range(NT):
                        ins = scaled(l, u, 0, zu[:, t, :], ACT.Gelu_apprx_tanh, D_B, t)
                    free_pair(ins, u)
                    if l == 0:
                        sc.wait_ge(mem_sem, 32)
                        for t in range(NT):
                            act_fn(mem_x[:, t, :], mem_x[:, t, :], ACT.Square,
                                   accum_out=ssq_mem[:, t:t + 1]).then_inc(mem_squared, 1)
                        sc.wait_ge(mem_squared, 2)
                elif name[0] in "IC":
                    c = int(name[1]) * u.width
                    dst = (ibuf if name[0] == "I" else cbuf)[:, :, c:c + u.width]
                    for t in range(NT):
                        ins = scaled(l, u, 0, dst[:, t, :], ACT.Identity, u.width, t)
                    free_pair(ins, u)
                elif name == "Z1":
                    decays(l)
                elif name == "Z0":
                    for t in range(NT):
                        ins = scaled(l, u, 0, zz[:, t, 0:COL], ACT.Silu, COL, t)
                    free_pair(ins, u)
                elif name == "KM":
                    free_pair(act_fn(km_t, pair_ch(u), ACT.Copy), u)
                elif name == "VM":
                    free_pair(act_fn(vm, pair(u), ACT.Copy), u)
                elif name[0] == "O" or name[0:2] == "D3":
                    wait_pair_freed(sc, l, u)
                    w = 2 if name[0] == "D" else 1 if name[1] == "M" else 0
                    squares(8 + 24 * l + 8 * w, int(name[-1]))
                elif name[0] == "U":
                    n = int(name[1]) * 4 + int(name[2])
                    if n == 0:
                        sc.wait_ge(*at("r_ready", l, 3))
                    if n >= 2:
                        sc.wait_ge(*at("h_sq_ready", l, n - 1))
                    for t in range(NT):
                        ins = scaled(l, u, 2, h_relu[:, n % 2, t * COL:t * COL + COL], ACT.Relu, COL, t)
                    free_pair(ins, u)

            def silu(l, s, g):
                sc.wait_ge(*at("conv_out", l, 3 * g + s + 1))
                d = (q_t[g], k_t, v_t)[s]
                signal(act_fn(d, d, ACT.Silu), "silu_out")

            def decays(l):
                u, w = U["Z1"], D_A - COL
                for t in range(NT):
                    ins = act_fn(db[:, t * 12:t * 12 + 12], pair(u)[:, t, w:w + 12], ACT.Identity,
                                 scale=r_norms[0][:, t:t + 1])
                    if t == 0:
                        chain.link(l, ins)
                signal(ins, "db_ready")
                sc.wait_ge(*at("att_p", l, 2))
                for t in range(NT):
                    ins = scaled(l, u, 0, zz[:, t, COL:], ACT.Silu, w, t)
                free_pair(ins, u)
                dbv = db.rearrange("p (t n) -> p t n", t=NT)
                sc.wait_ge(*at("db_ready", l, 1))
                signal(act_fn(beta.rearrange("p (t n) -> p t n", t=NT), dbv[:, :, 6:12], ACT.Exp, scale=-1.0), "beta_exp")
                signal(act_fn(eal, al, ACT.Exp), "eal_ready")
                sc.wait_ge(*at("abs_ready", l, 1))
                chain.link(l, act_fn(t_abs, t_abs, ACT.Exp, scale=-1.0))
                if l == 0:
                    sc.wait_ge(const_rest_sem, 16)
                signal(act_fn(t_abs, t_abs, ACT.Ln, bias=ones[:, 0:1]), "dec_ln")

            def memory(l, c):
                if l == 0 and c == 0:
                    sc.wait_ge(r_mem_ready, 1)
                sc.wait_ge(mem_landed[c % 2], 32 * l + 16 * (c // 2 + 1))
                for t in range(NT):
                    ins = act_fn(mem_c[c % 2][:, t, :], mem_c[c % 2][:, t, :], ACT.Identity, scale=r_mem[:, t:t + 1])
                    if t == 0:
                        chain.link(l, ins)
                signal(ins, "mem_scaled")

            def group_start(l, g):
                ahead(l, piece_before[("ssq", g)])
                sc.wait_ge(*at("silu_out", l, 3 * g + 2))
                if g == 0:
                    wait_freed(sc, l, ("aoT", 1, 1))
                else:
                    wait_freed(sc, l, ("kk", g - 1, 1))
                    wait_full(sc, l, ("kq", g - 1, 1))
                for src, dst in ((q_t[g], sqq), (k_t, sqk)):
                    signal(act_fn(dst.rearrange("p a b -> p (a b)"), src.rearrange("p a b -> p (a b)"), ACT.Square),
                           "sqs")

            def group_mid(l, g):
                for t in range(NT):
                    copy_out(l, ("kn", g, t), kn_t[:, t * GH:t * GH + GH, :], GH * P, split=P)
                if g == 0:
                    ahead(l, piece_before["gcum"])
                    wait_freed(sc, l, "gcum")
                    signal(act_fn(eg, gcum, ACT.Exp), "eg_ready")
                ahead(l, piece_before[("grow", g, 1)])
                for t in range(NT):
                    wait_freed(sc, l, ("grow", g, t))
                    for h in range(GH):
                        i, c = t * GH + h, ci(t, g, h)
                        chain.run(act_fn(dec[:, i, :], dec[:, i, :], ACT.Exp, scale=-1.0, bias=gcum[:, c:c + 1]))
                        ins = act_fn(dec_t[:, i, :], dec_t[:, i, :], ACT.Exp, bias=ngcum[:, c:c + 1])
                        if h < GH - 1:
                            chain.run(ins)
                    signal(ins, "dec_val")
                sc.wait_ge(*at("kd_arg", l, g + 1))
                signal(act_fn(egl, glast, ACT.Exp), "egl_ready")

            def values(l, g):
                sc.wait_ge(*at("beta_ready", l, 1))
                for t in range(NT):
                    b = reach(l, ("v", g, t))
                    for h in range(GH):
                        c = ci(t, g, h)
                        ins = act_fn(vb[:, t * GH + h, :], b[:, h * P:h * P + P], ACT.Identity, scale=beta[:, c:c + 1])
                    free(ins, ("v", g, t))

            def group_inverse(l, g):
                for lev in range(1, LEVELS):
                    if lev == (3, 5)[g]:
                        values(l, g)
                    if lev == 3 and g == 1:
                        group_out(l, 0)
                    for t in range(NT):
                        r = rmat[:, t * GH:t * GH + GH, :]
                        if lev == LEVELS - 1:
                            copy_out(l, ("R", g, lev, t), r[:, :, P // 2:], GH * P // 2, split=P // 2)
                        else:
                            copy_out(l, ("R", g, lev, t), r, GH * P, split=P)
                    if g == 1 and lev < 4:
                        norm_hi(l, 3, range(4 * lev, 4 * lev + 4))
                        if lev < 3:
                            memory(l, lev + 1)

            def group_scan(l, g):
                reach(l, ("U", g, LEVELS - 1, 1))
                sc.wait_ge(*at("beg_ready", l, 1))
                sc.wait_ge(*at("egl_ready", l, g + 1))
                for t, f in ((0, egl), (1, beg)):
                    for h in range(GH):
                        c = h if t == 0 else ci(1, g, h)
                        ins = act_fn(ksc[:, t * GH + h, :], kn[:, t * GH + h, :], ACT.Identity, scale=f[:, c:c + 1])
                        if h < GH - 1:
                            chain.run(ins)
                        else:
                            signal(ins, "ksc_ready")
                copy_out(l, ("vn0", g), vn[:, 0:GH, :], GH * P, split=P)
                copy_out(l, ("w1", g), w1, GH * P, scale=-1.0, split=P)
                copy_out(l, ("s1", g), s1, GH * P, split=P)
                copy_out(l, ("vn1", g), vn[:, GH:, :], GH * P, split=P)
                b = reach(l, ("qs", g))
                for h in range(GH):
                    c = ci(1, g, h)
                    ins = act_fn(qs[:, h, :], b[:, h * P:h * P + P], ACT.Identity, scale=eg[:, c:c + 1])
                free(ins, ("qs", g))

            def group_out(l, g):
                ahead(l, piece_before[("oT", g, 0)])
                for h in range(GH):
                    hi_part(l, ("oT", g, h), act["B"][0][:, g * GH + h, :], "gdn_hi", scale=gain("gdn", 0))

            def relus(l, t):
                width = (t + 1) * P
                per = COL // width
                for n in range(IDX_HEADS // per):
                    k = n + (4 if t else 0)
                    name = ("score", t, n)
                    b = reach(l, name)
                    if k >= 2:
                        sc.wait_ge(*at("relu_used", l, k - 1))
                    free(act_fn(relu[:, k % 2, :], b, ACT.Relu), name)

            def att_softmax(l, t):
                width = (t + 1) * P
                ahead(l, piece_before[("logit", t, 2 if t else 1)])
                sc.wait_ge(*at("logits_ready", l, t + 1))
                for h in range(SA_HEADS):
                    signal(act_fn(logit[:, h, 0:width], logit[:, h, 0:width], ACT.Exp,
                                  bias=smax[:, t * 6 + h:t * 6 + h + 1], accum_out=ssum[:, t * 6 + h:t * 6 + h + 1]),
                           "att_exp")

            def att_values(l, t):
                ahead(l, piece_before[("pT", t, 0, 0)])
                for s in range(t + 1):
                    for n in range(2):
                        copy_out(l, ("pT", t, s, n), p_t[:, n * GH:n * GH + GH, s, :], GH * P, split=P)
                for n in range(2):
                    hi_part(l, ("aoT", t, n), act["B"][0][:, 10 + n * GH:10 + n * GH + GH, t * P:t * P + P], "att_hi")

            def hidden_hi(l, q, j):
                for half in range(2):
                    hi_part(l, ("hT", q, j, half), act["B"][0][:, 4 * j + 2 * half:4 * j + 2 * half + 2, :], "ffn_hi")

            def layer(l):
                norm_hi(l, 0, range(12, KT))
                if l == 0:
                    for j in range(4):
                        sc.wait_ge(x_sem[j], 16)
                        squares(0, j)
                if l > 0:
                    wait_freed(sc, l - 1, ("norm", 2, KT - 1))
                for i in range(2):
                    n = PAR_ROWS[i]
                    copy_out(l, ("par", i), par[:, i, 0:n], n)
                for i in range(2):
                    wait_freed(sc, l, ("par", i))
                copy_out(l, "sgw", sgw_t[:], SG_GROUPS * P, split=P)
                for i in range(SG_GROUPS):
                    hi_part(l, ("bT", i), act["B"][0][:, 6 + i, :], "gate_hi")
                copy_out(l, "ikT", ik_t, SEQ)
                for t in range(NT):
                    for half in range(2):
                        copy_out(l, ("iqT", t, half), iq_t[:, t, 4 * half:4 * half + 4, :], COL, split=P)
                relus(l, 0)
                relus(l, 1)
                copy_out(l, "ckT", ck_t, SEQ)
                for n in range(3):
                    copy_out(l, ("cqT", n), cq_t[:, 2 * n:2 * n + 2, :], COL, split=SEQ)
                att_softmax(l, 0)
                att_values(l, 0)
                att_softmax(l, 1)
                att_values(l, 1)
                for g in range(2):
                    group_start(l, g)
                    group_mid(l, g)
                    if g == 1:
                        memory(l, 0)
                        norm_hi(l, 3, range(4))
                        memory(l, 1)
                    group_inverse(l, g)
                    group_scan(l, g)
                group_out(l, 1)
                norm_hi(l, 1, range(KT))
                for t in range(NT):
                    ahead(l, piece_before[("xlogit", t, 1)])
                    sc.wait_ge(*at("xlog_ready", l, t + 1))
                    for h in range(MEM_HEADS):
                        c, name = t * MEM_HEADS + h, ("xlogit", t, h // 2)
                        b = bank_of(name)[:, h % 2 * MEM_LEN:(h % 2 + 1) * MEM_LEN]
                        ins = act_fn(xlogit[:, t, h, :], b, ACT.Exp, scale=SCALE, bias=xmax[:, c:c + 1],
                                     accum_out=xsum[:, c:c + 1])
                        if h % 2:
                            free(ins, name)
                        else:
                            signal(ins, "xexp")
                for t in range(NT):
                    for s in range(NT):
                        copy_out(l, ("xpT", t, s), xp_t[:, :, s, t * P:t * P + P], COL, split=P)
                for h in range(MEM_HEADS):
                    hi_part(l, ("xo", h), act["B"][0][:, h, :], "xat_hi")
                norm_hi(l, 2, range(KT))
                for q in range(4):
                    for j in range(4):
                        hidden_hi(l, q, j)
                if l < DEPTH - 1:
                    norm_hi(l + 1, 0, range(12))
                ahead(l, PIECES - 1)
                nxt[0] -= PIECES

            sc.wait_ge(mix_turned, 1)
            act_fn(mix_gain, psum[:, 3, 0:DEPTH * KT], ACT.Copy).then_inc(mix_ready, 1)
            sc.wait_ge(mix_ready, 1)
            norm_hi(0, 0, range(4))
            ahead(0, -1)
            norm_hi(0, 0, range(4, 12))
            for l in range(DEPTH):
                layer(l)

        @block.vector
        def _(dve):
            V = nc.vector
            chain = Chain(dve, "vector_done", 0)
            nxt = [0]

            def ahead(l, piece):
                while nxt[0] <= piece + RING - 1:
                    g = nxt[0]
                    nxt[0] += 1
                    if l * PIECES + g < DEPTH * PIECES:
                        s, w = g % RING, unit_of(g).width
                        dve.wait_ge(hi_ready, l * PIECES + g + 1)
                        V.tensor_tensor(w_lo[:, s, :, 0:w], w_raw[:, s, :, 0:w], w_hi[:, s, :, 0:w].bitcast(F32),
                                        ALU.subtract).then_inc(lo_ready, 1)
                    if g - (RING - 1) in ends:
                        result(l, ends[g - (RING - 1)])
                    for step in range(CONV_K):
                        u = ends.get(g - (RING - 1) - step)
                        if u and u.name in CONV:
                            conv(l, u, *CONV[u.name], step)

            def result(l, u):
                name = u.name
                if name == "B1":
                    gate_norm(l)
                elif name == "Z1":
                    decays(l)
                elif name == "QM":
                    rms_row(l, 1)
                    wait_unit(dve, l, u)
                    free_pair(V.tensor_tensor(qm_t, pair_ch(u), each(r_row, MEM_HEADS), ALU.mult), u)
                elif name[0] in "OD":
                    wait_unit(dve, l, u)
                    j = int(name[-1])
                    c = slice(j * COL, j * COL + COL)
                    free_pair(V.tensor_tensor(x_res[:, :, c], x_res[:, :, c], pair(u), ALU.add), u)

            def reach(l, name):
                ahead(l, piece_before[name])
                wait_full(dve, l, name)
                return bank_of(name)

            def link(l, ins):
                chain.link(l, ins)

            def rsqrt(l, n, dst):
                y, a, b = y_in[:, 0:n], y_a[:, 0:n], y_b[:, 0:n]
                link(l, V.tensor_scalar(a.bitcast(I32), y.bitcast(I32), 1, None, ALU.logical_shift_right))
                link(l, V.tensor_scalar(dst.bitcast(I32), a.bitcast(I32), -1.0, float(0x5f3759df), ALU.mult, ALU.add))
                for _ in range(3):
                    link(l, V.tensor_tensor(a, dst, dst, ALU.mult))
                    link(l, V.scalar_tensor_tensor(out=b, in0=a, scalar=-0.5, in1=y, op0=ALU.mult, op1=ALU.mult))
                    link(l, V.scalar_tensor_tensor(out=dst, in0=b, scalar=1.5, in1=dst, op0=ALU.add, op1=ALU.mult))

            def lo_part(l, name, dst, hi, sig, count, scale=None):
                ahead(l, piece_before[name])
                dve.wait_ge(*at(sig, l, count))
                b = bank_of(name)[:, 0:int(np.prod(dst.shape[1:]))]
                if len(dst.shape) == 3:
                    b = b.rearrange("p (a b) -> p a b", b=dst.shape[2])
                hi = hi.bitcast(F32)
                if scale is None:
                    ins = V.tensor_tensor(dst, b, hi, ALU.subtract)
                else:
                    ins = V.scalar_tensor_tensor(out=dst, in0=b, scalar=scale, in1=hi, op0=ALU.mult, op1=ALU.subtract)
                free(ins, name)

            def norm_r(l, w):
                dve.wait_ge(*at("ssq_ready", l, 8 * w))
                link(l, V.tensor_reduce(y_a[:, 0:2], ssq.rearrange("p (t j) -> p t j", j=4), AX.X, ALU.add))
                link(l, V.tensor_scalar(y_in[:, 0:2], y_a[:, 0:2], 1.0 / D_MODEL, EPS, ALU.mult, ALU.add))
                rsqrt(l, 2, r_out)
                signal(V.tensor_copy(r_norms[w], r_out), "r_ready")
                dve.wait_ge(*at("r_ready", l, w + 1))

            def rms_diag(l, w):
                for t in range(NT):
                    ins = V.tensor_scalar(diag[:, t, :], ident, r_norms[w][:, t:t + 1], None, ALU.mult)
                    if t == 0:
                        link(l, ins)
                signal(ins, "diag_ready")

            def rms_row(l, w):
                for t in range(NT):
                    name = ("row", w, t)
                    wait_full(dve, l, name)
                    free(V.tensor_copy(r_row[:, t * P:t * P + P], bank_of(name)[:, 0:P]), name)
                for t in range(NT):
                    wait_freed(dve, l, ("row", w, t))

            def norm_lo(l, w, kts):
                hi, lo = act["A"]
                for kt in kts:
                    name, at_l, n, g = norm_use(l, w, kt)
                    if at_l >= 0:
                        ahead(at_l, piece_before[name])
                    dve.wait_ge(*at("act_hi", at_l, n))
                    free(V.scalar_tensor_tensor(out=lo[:, kt, :], in0=bank_of(name)[:, 0:SEQ], scalar=g,
                                                in1=hi[:, kt, :].bitcast(F32), op0=ALU.mult, op1=ALU.subtract), name)

            def gate_norm(l):
                wait_pair_freed(dve, l, U["B1"])
                signal(V.tensor_scalar(mean, mean, -1.0 / D_B, None, ALU.mult), "gate_nmean")
                ahead(l, U["B0"].first)
                dve.wait_ge(*at("gate_var", l, 2))
                link(l, V.tensor_scalar(y_in[:, 0:2], rstd, 1.0 / D_B, EPS, ALU.mult, ALU.add))
                rsqrt(l, 2, rstd)
                for t in range(NT):
                    signal(V.tensor_scalar(zv[:, t, :], zv[:, t, :], mean[:, t:t + 1], rstd[:, t:t + 1], ALU.add,
                                           ALU.mult), "gate_norm")

            def gate_apply(l):
                for t in range(NT):
                    b = reach(l, ("sg", t))
                    if t == 0:
                        wait_pair_freed(dve, l, U["B0"])
                    for i in range(SG_GROUPS):
                        c = slice(i * P, i * P + P)
                        ins = V.scalar_tensor_tensor(out=zu[:, t, c], in0=b[:, c], scalar=gain("sg_b", i),
                                                     in1=zu[:, t, c], op0=ALU.add, op1=ALU.mult)
                    free(ins, ("sg", t))

            def rope(l, buf, ta, tb, heads, half, cos, sin, n, units_, pieces=()):
                for u in units_:
                    ahead(l, u.first + u.pieces - 1)
                    wait_pair_freed(dve, l, u)
                w = heads * 2 * half

                def view(a, t):
                    return a[:, t, 0:w].rearrange("p (h a d) -> p h a d", a=2, d=half)

                for t in range(NT):
                    c = cst(cos, NT)[:, t, :].unsqueeze(1).unsqueeze(1).to_broadcast([P, heads, 2, half])
                    link(l, V.tensor_tensor(view(ta, t), view(buf, t), c, ALU.mult))
                    dve.wait_ge(*at("rope_b", l, n + t + 1))
                    x_, a_, b_ = view(buf, t), view(ta, t), view(tb, t)
                    chain.run(V.tensor_tensor(x_[:, :, 0, :], a_[:, :, 0, :], b_[:, :, 1, :], ALU.subtract))
                    signal(V.tensor_tensor(x_[:, :, 1, :], a_[:, :, 1, :], b_[:, :, 0, :], ALU.add), "rope_done")
                    if pieces:
                        ahead(l, pieces[t])
                chain.settle(l)

            def index_rope(l):
                rope(l, ibuf, tmp_a, tmp_b, IDX_HEADS + 1, 32, "cos_i", "sin_i", 0, [U["I0"], U["I1"], U["I2"]],
                     [U["C0"].first, U["C0"].first + 1])
                dve.wait_ge(*at("rope_done", l, 2))
                s = IDX_HEADS * IDX_DIM
                chain.run(V.tensor_scalar(iw.rearrange("p (t h) -> p t h", t=NT), ibuf[:, :, s + IDX_DIM:],
                                          IDX_HEADS ** -0.5 * IDX_DIM ** -0.5, None, ALU.mult))
                chain.run(V.tensor_copy(ik2[:, :, 0:64], ibuf[:, :, s:s + IDX_DIM]))
                signal(V.tensor_copy(ik2[:, :, 64:128], ibuf[:, :, s:s + IDX_DIM]), "rope_done")

            def scores(l, t):
                width = (t + 1) * P
                per = COL // width
                d = score[:, t, 0:width]
                for n in range(IDX_HEADS // per):
                    k = n + (4 if t else 0)
                    ahead(l, piece_before[("score", t, n)])
                    wait_freed(dve, l, ("score", t, n))
                    for i in range(per):
                        h = score_head(n, i, per)
                        src, wt = relu[:, k % 2, i * width:(i + 1) * width], iw[:, t * 16 + h:t * 16 + h + 1]
                        if h == 0:
                            chain.settle(l)
                            ins = V.tensor_scalar(d, src, wt, None, ALU.mult)
                        else:
                            ins = V.scalar_tensor_tensor(out=d, in0=src, scalar=wt, in1=d, op0=ALU.mult, op1=ALU.add)
                        if i < per - 1:
                            link(l, ins)
                        else:
                            signal(ins, "relu_used")
                            dve.wait_ge(*at("relu_used", l, k + 1))
                signal(V.tensor_copy(work[:, t, 0:width], d), "score_done")

            def topk(l, t, pieces):
                width = (t + 1) * P
                w = work[:, t, 0:width]
                dve.wait_ge(*at("masked", l, t + 1))
                for r in range(TOPK // 8):
                    m = max8[:, (r % 2) * 8:(r % 2) * 8 + 8]
                    link(l, V.max(m, w))
                    link(l, V.match_replace(w, m, w, TAKEN))
                    if r in pieces:
                        ahead(l, U["Q0"].first + pieces[r])
                signal(V.tensor_scalar(mbias[:, t, 0:width], w, -2e38, -OFF, ALU.is_gt, ALU.mult), "topk_done")

            def att_logits(l, t):
                width = (t + 1) * P
                per = 3 if t == 0 else 2
                if t == 0:
                    dve.wait_ge(*at("mask_ready", l, 1))
                else:
                    dve.wait_ge(*at("topk_done", l, 2))
                for n in range(SA_HEADS // per):
                    name = ("logit", t, n)
                    b = reach(l, name)
                    free(V.scalar_tensor_tensor(out=logit[:, n * per:(n + 1) * per, 0:width],
                                                in0=b[:, 0:per * width].rearrange("p (a b) -> p a b", b=width),
                                                scalar=SCALE, in1=each(mbias[:, t, 0:width], per),
                                                op0=ALU.mult, op1=ALU.add), name)
                for n in range(SA_HEADS // per):
                    wait_freed(dve, l, ("logit", t, n))
                c = slice(t * 6, t * 6 + 6)
                link(l, V.tensor_reduce(smax[:, c], logit[:, :, 0:width], AX.X, ALU.max))
                signal(V.tensor_scalar(smax[:, c], smax[:, c], -1.0, None, ALU.mult), "logits_ready")

            def att_norm(l, t):
                width, c = (t + 1) * P, slice(t * 6, t * 6 + 6)
                ahead(l, piece_before[("logit", t, 1 + t)] + 1)
                dve.wait_ge(*at("att_exp", l, 6 * (t + 1)))
                link(l, V.reciprocal(sinv[:, c], ssum[:, c]))
                for h in range(SA_HEADS):
                    ins = V.tensor_scalar(logit[:, h, 0:width], logit[:, h, 0:width], sinv[:, t * 6 + h:t * 6 + h + 1],
                                          None, ALU.mult)
                    if h < SA_HEADS - 1:
                        chain.run(ins)
                chain.settle(l)
                signal(ins, "att_p")

            def att_lo(l, t):
                hi, lo = act["B"]
                for n in range(2):
                    k, c = slice(10 + n * GH, 10 + n * GH + GH), slice(t * P, t * P + P)
                    lo_part(l, ("aoT", t, n), lo[:, k, c], hi[:, k, c], "att_hi", 2 * t + n + 1)

            def conv(l, u, s, g, step):
                if step == 0:
                    if s == 0 and g == 0:
                        dve.wait_ge(*at("rope_done", l, 5))
                        chain.run(V.tensor_scalar(x_pad[:, :, 0:CONV_K - 1],
                                                  const[:, 0:9].rearrange("p (a b) -> p a b", b=3), 0.0, None,
                                                  ALU.mult))
                    wait_unit(dve, l, u)
                    free_pair(V.tensor_tensor(x_pad[:, :, CONV_K - 1:], pair_ch(u)[:, 0:GH, :], each(r_row, GH),
                                              ALU.mult), u)
                    wait_pair_freed(dve, l, u)
                chain.settle(l)
                d, j = (q_t[g], k_t, v_t)[s], CONV_K - 1 - step
                for h in range(GH):
                    w = conv_tap(j, s * GDN_HEADS + g * GH + h)
                    src = x_pad[:, h, j:j + SEQ]
                    if step == 0:
                        ins = V.tensor_scalar(d[:, h, :], src, w, None, ALU.mult)
                    else:
                        ins = V.scalar_tensor_tensor(out=d[:, h, :], in0=src, scalar=w, in1=d[:, h, :],
                                                     op0=ALU.mult, op1=ALU.add)
                    if j == 0 and h == GH - 1:
                        signal(ins, "conv_out")
                    else:
                        chain.run(ins)

            def decays(l):
                dve.wait_ge(*at("db_ready", l, 1))
                for t in range(NT):
                    chain.run(V.tensor_tensor(t_ln[:, t * 6:t * 6 + 6], db[:, t * 12:t * 12 + 6], dtb, ALU.add))
                chain.settle(l)
                signal(V.scalar_tensor_tensor(out=t_abs, in0=t_ln, scalar=-1.0, in1=t_ln, op0=ALU.mult, op1=ALU.max),
                       "abs_ready")
                dve.wait_ge(*at("beta_exp", l, 1))
                link(l, V.tensor_scalar(beta, beta, 1.0, None, ALU.add))
                signal(V.reciprocal(beta, beta), "beta_ready")
                dve.wait_ge(*at("dec_ln", l, 1))
                link(l, V.scalar_tensor_tensor(out=gate, in0=t_ln, scalar=0.0, in1=t_abs, op0=ALU.max, op1=ALU.add))
                dve.wait_ge(*at("eal_ready", l, 1))
                chain.run(V.scalar_tensor_tensor(out=gate[:, 0:6], in0=gate[:, 0:6], scalar=-1.0, in1=eal,
                                                 op0=ALU.mult, op1=ALU.mult))
                chain.settle(l)
                signal(V.scalar_tensor_tensor(out=gate[:, 6:12], in0=gate[:, 6:12], scalar=-1.0, in1=eal,
                                              op0=ALU.mult, op1=ALU.mult), "gate_g")

            def group_sums(l, g):
                b = reach(l, ("ssq", g))
                if g == 0:
                    wait_freed(dve, l, ("aoT", 1, 1))
                free(V.tensor_scalar(y_in[:, 0:12], b[:, 0:12], EPS, None, ALU.add), ("ssq", g))
                wait_freed(dve, l, ("ssq", g))
                rsqrt(l, 12, r_qk[g])

            def group_mid(l, g):
                for t in range(NT):
                    b = reach(l, ("k", g, t))
                    for h in range(GH):
                        i = t * GH + h
                        ins = V.tensor_scalar(kn[:, i, :], b[:, h * P:h * P + P], r_qk[g][:, NC + i:NC + i + 1], None,
                                              ALU.mult)
                        if h < GH - 1:
                            chain.run(ins)
                    free(ins, ("k", g, t))
                if g == 0:
                    b = reach(l, "gcum")
                    chain.run(V.tensor_scalar(ngcum, b[:, 0:12], -1.0, None, ALU.mult))
                    free(V.tensor_copy(gcum, b[:, 0:12]), "gcum")
                    wait_freed(dve, l, "gcum")
                    dve.wait_ge(*at("eg_ready", l, 1))
                    signal(V.tensor_tensor(beg, beta, eg, ALU.mult), "beg_ready")
                for t in range(NT):
                    b = reach(l, ("grow", g, t))[:, 0:GH * P].rearrange("p (a b) -> p a b", b=P)
                    r = slice(t * GH, t * GH + GH)
                    if t == 0:
                        chain.run(V.tensor_copy(glast.unsqueeze(2), b[:, :, P - 1:P]))
                    chain.run(V.tensor_tensor(dec[:, r, :], b, each(cst("strict"), GH), ALU.add))
                    free(V.tensor_tensor(dec_t[:, r, :], b, each(cst("incl"), GH), ALU.subtract), ("grow", g, t))
                chain.settle(l)
                signal(V.tensor_tensor(glast, glast, gcum[:, g * GH:g * GH + GH], ALU.subtract), "kd_arg")
                for t in range(NT):
                    b = reach(l, ("kk", g, t))
                    dve.wait_ge(*at("dec_val", l, 2 * g + t + 1))
                    for h in range(GH):
                        i, c = t * GH + h, ci(t, g, h)
                        ins = V.scalar_tensor_tensor(out=amat[:, i, :], in0=b[:, h * P:h * P + P],
                                                     scalar=beta[:, c:c + 1], in1=dec[:, i, :], op0=ALU.mult,
                                                     op1=ALU.mult)
                        if h < GH - 1:
                            chain.run(ins)
                    free(ins, ("kk", g, t))
                for t in range(NT):
                    b = reach(l, ("kq", g, t))[:, 0:GH * P].rearrange("p (a b) -> p a b", b=P)
                    r = slice(t * GH, t * GH + GH)
                    free(V.tensor_tensor(dec_t[:, r, :], b, dec_t[:, r, :], ALU.mult), ("kq", g, t))

            def group_inverse(l, g):
                dve.wait_ge(*at("off_ready", l, g * LEVELS + 1))
                signal(V.tensor_tensor(tmat, each(ident, NC), aoff, ALU.subtract), "t_ready")
                for t in range(NT):
                    b = reach(l, ("R", g, 0, t))[:, 0:GH * P].rearrange("p (a b) -> p a b", b=P)
                    free(V.tensor_tensor(umat[:, t * GH:t * GH + GH, :], each(ident, GH), b, ALU.subtract), ("R", g, 0, t))
                dve.wait_ge(*at("t_ready", l, g + 1))
                for lev in range(1, LEVELS):
                    if g == 1 and lev == 3:
                        group_gate(l, 0)
                        group_out(l, 0)
                    if g == 1 and lev < 4:
                        norm_lo(l, 3, range(4 * lev, 4 * lev + 4))
                    for t in range(NT):
                        r = slice(t * GH, t * GH + GH)
                        for name, m in (("U", umat), ("T", tmat)):
                            if name == "T" and lev == LEVELS - 1:
                                continue
                            if lev > 1 or name == "U":
                                wait_freed(dve, l, (name, g, lev - 1, t))
                            b = packed(reach(l, (name, g, lev, t)), lev, GH)
                            d = half(m[:, r, :], lev, int(name == "U"))
                            free(V.tensor_tensor(d, d, b, ALU.subtract), (name, g, lev, t))

            def group_scan(l, g):
                b = reach(l, ("o0", g))[:, 0:GH * P].rearrange("p (a b) -> p a b", b=P)
                free(V.tensor_copy(obuf[:, 0:GH, :], b), ("o0", g))
                b = reach(l, ("o1", g))[:, 0:GH * P].rearrange("p (a b) -> p a b", b=P)
                wait_freed(dve, l, ("qs", g))
                free(V.tensor_tensor(obuf[:, GH:, :], b, qs, ALU.add), ("o1", g))
                wait_freed(dve, l, ("o0", g))
                wait_freed(dve, l, ("o1", g))
                link(l, V.tensor_tensor(rmat, obuf, obuf, ALU.mult))
                link(l, V.tensor_reduce(y_b[:, 0:NC], rmat, AX.X, ALU.add))
                link(l, V.tensor_scalar(o_c, r_qk[g][:, 0:NC], SCALE, None, ALU.mult))
                link(l, V.tensor_tensor(y_a[:, 0:NC], o_c, o_c, ALU.mult))
                link(l, V.scalar_tensor_tensor(out=y_in[:, 0:NC], in0=y_b[:, 0:NC], scalar=1.0 / HEAD,
                                               in1=y_a[:, 0:NC], op0=ALU.mult, op1=ALU.mult))
                link(l, V.tensor_scalar(y_in[:, 0:NC], y_in[:, 0:NC], EPS, None, ALU.add))
                rsqrt(l, NC, r_o)
                link(l, V.tensor_tensor(o_f, o_c, r_o, ALU.mult))

            def group_gate(l, g):
                ahead(l, U["Z0"].first + 7)
                for name in ("Z0", "Z1"):
                    wait_pair_freed(dve, l, U[name])
                for i in range(NC):
                    t, h = i // GH, g * GH + i % GH
                    ins = V.scalar_tensor_tensor(out=obuf[:, i, :], in0=obuf[:, i, :], scalar=o_f[:, i:i + 1],
                                                 in1=zz[:, t, h * P:h * P + P], op0=ALU.mult, op1=ALU.mult)
                    if i < NC - 1:
                        chain.run(ins)
                chain.settle(l)
                signal(ins, "o_ready")

            def group_out(l, g):
                hi, lo = act["B"]
                for h in range(GH):
                    k = g * GH + h
                    lo_part(l, ("oT", g, h), lo[:, k, :], hi[:, k, :], "gdn_hi", k + 1, scale=gain("gdn", 0))

            def hidden_lo(l, q, j):
                hi, lo = act["B"]
                for half in range(2):
                    k = slice(4 * j + 2 * half, 4 * j + 2 * half + 2)
                    lo_part(l, ("hT", q, j, half), lo[:, k, :], hi[:, k, :], "ffn_hi", (q * 4 + j) * 2 + half + 1)

            def layer(l):
                norm_lo(l, 0, range(12, KT))
                norm_r(l, 0)
                if l == 0:
                    dve.wait_ge(const_rest_sem, 16)
                ahead(l, piece_before["sgw"])
                wait_full(dve, l, "sgw")
                rms_diag(l, 0)
                ahead(l, piece_before[("row", 0, 0)])
                rms_row(l, 0)
                if l == 0:
                    dve.wait_ge(mem_squared, 2)
                    link(l, V.tensor_scalar(y_in[:, 0:2], ssq_mem, 1.0 / D_MODEL, EPS, ALU.mult, ALU.add))
                    rsqrt(l, 2, r_out)
                    V.tensor_copy(r_mem, r_out).then_inc(r_mem_ready, 1)
                for i in range(2):
                    wait_freed(dve, l, ("par", i))
                gate_apply(l)
                hi, lo = act["B"]
                for i in range(SG_GROUPS):
                    lo_part(l, ("bT", i), lo[:, 6 + i, :], hi[:, 6 + i, :], "gate_hi", i + 1)
                index_rope(l)
                scores(l, 0)
                scores(l, 1)
                topk(l, 0, {2: 0, 5: 1})
                rope(l, cbuf, rope_a, rope_b, SA_HEADS + 1, 64, "cos_h", "sin_h", 2, [U["C0"], U["C1"]],
                     [U["Q0"].first + 2, U["Q0"].first + 3])
                att_logits(l, 0)
                topk(l, 1, {0: 6, 1: 7, 3: 8, 5: 9})
                att_norm(l, 0)
                att_lo(l, 0)
                att_logits(l, 1)
                att_norm(l, 1)
                att_lo(l, 1)
                for g in range(2):
                    group_sums(l, g)
                    group_mid(l, g)
                    if g == 1:
                        norm_lo(l, 3, range(4))
                    group_inverse(l, g)
                    group_scan(l, g)
                group_gate(l, 1)
                group_out(l, 1)
                norm_lo(l, 1, range(KT))
                norm_r(l, 1)
                rms_diag(l, 1)
                for t in range(NT):
                    for n in range(2):
                        b = reach(l, ("xlogit", t, n)).rearrange("p (a b) -> p a b", b=MEM_LEN)
                        chain.run(V.tensor_reduce(xmax[:, t * 4 + 2 * n:t * 4 + 2 * n + 2], b, AX.X, ALU.max))
                    chain.settle(l)
                    c = slice(t * 4, t * 4 + 4)
                    signal(V.tensor_scalar(xmax[:, c], xmax[:, c], -SCALE, None, ALU.mult), "xlog_ready")
                for t in range(NT):
                    c = slice(t * 4, t * 4 + 4)
                    dve.wait_ge(*at("xexp", l, 2 * t + 2))
                    for n in range(2):
                        wait_freed(dve, l, ("xlogit", t, n))
                    link(l, V.reciprocal(xinv[:, c], xsum[:, c]))
                    for h in range(MEM_HEADS):
                        ins = V.tensor_scalar(xlogit[:, t, h, :], xlogit[:, t, h, :],
                                              xinv[:, t * 4 + h:t * 4 + h + 1], None, ALU.mult)
                        if h < MEM_HEADS - 1:
                            chain.run(ins)
                    chain.settle(l)
                    signal(ins, "xp_ready")
                for h in range(MEM_HEADS):
                    lo_part(l, ("xo", h), lo[:, h, :], hi[:, h, :], "xat_hi", h + 1)
                norm_lo(l, 2, range(KT))
                norm_r(l, 2)
                for q in range(4):
                    for j in range(4):
                        hidden_lo(l, q, j)
                if l < DEPTH - 1:
                    norm_lo(l + 1, 0, range(12))
                ahead(l, PIECES - 1)
                nxt[0] -= PIECES

            dve.wait_ge(const_sem, 16)
            dve.wait_ge(mix_ready, 1)
            norm_lo(0, 0, range(4))
            ahead(0, -1)
            norm_lo(0, 0, range(4, 12))
            for j in range(4):
                dve.wait_ge(x_sem[j], 16)
            for l in range(DEPTH):
                layer(l)
            l = DEPTH
            dve.wait_ge(*at("ssq_ready", l, 0))
            link(l, V.tensor_reduce(y_a[:, 0:2], ssq.rearrange("p (t j) -> p t j", j=4), AX.X, ALU.add))
            link(l, V.tensor_scalar(y_in[:, 0:2], y_a[:, 0:2], 1.0 / D_MODEL, EPS, ALU.mult, ALU.add))
            rsqrt(l, 2, r_out)
            dve.wait_ge(fin_row_sem, 16)
            for t in range(NT):
                V.scalar_tensor_tensor(out=fin[:, t, :], in0=x_res[:, t, :], scalar=r_out[:, t:t + 1], in1=fin_row,
                                       op0=ALU.mult, op1=ALU.mult).then_inc(fin_sem, 1)

        @block.gpsimd
        def _(pool):
            G = nc.gpsimd
            chain = Chain(pool, "gpsimd_done", 0)

            def rope(l, buf, tb, heads, half, sin, n, units_):
                for u in units_:
                    wait_pair_freed(pool, l, u)
                w = heads * 2 * half
                for t in range(NT):
                    s = cst(sin, NT)[:, t, :].unsqueeze(1).unsqueeze(1).to_broadcast([P, heads, 2, half])
                    signal(G.tensor_tensor(tb[:, t, 0:w].rearrange("p (h a d) -> p h a d", a=2, d=half),
                                           buf[:, t, 0:w].rearrange("p (h a d) -> p h a d", a=2, d=half), s, ALU.mult),
                           "rope_b")

            def triangle_rows(l, g):
                if g == 0:
                    wait_freed(pool, l, ("aoT", 1, 1))
                    pool.wait_ge(*at("gate_g", l, 1))
                else:
                    wait_full(pool, l, ("o1", g - 1))
                for t in range(NT):
                    for h in range(GH):
                        c = ci(t, g, h)
                        ins = G.tensor_scalar(trig[:, t * GH + h, :], cst("tri"), gate[:, c:c + 1], None, ALU.mult)
                        if t * GH + h < NC - 1:
                            chain.run(ins)
                chain.settle(l)
                signal(ins, "trig_ready")

            def off_diagonals(l, g):
                for lev in range(LEVELS):
                    if lev == 0:
                        for t in range(NT):
                            wait_freed(pool, l, ("kk", g, t))
                    else:
                        wait_full(pool, l, ("R", g, lev - 1, 1))
                        if lev == 1:
                            pool.wait_ge(*at("t_ready", l, g + 1))
                    signal(G.tensor_tensor(aoff, amat, each(level[:, lev, :], NC), ALU.mult), "off_ready")

            pool.wait_ge(const_rest_sem, 16)
            for l in range(DEPTH):
                pool.wait_ge(*at("rows_landed", l, 48))
                signal(G.affine_select(out=sgw[:], in_=sgw[:], compare_op=ALU.is_ge, fill=0.0, base=0,
                                       pattern=[[0, SG_GROUPS], [-1, P]], channel_multiplier=1), "gate_w")
                for t in range(NT):
                    pool.wait_ge(*at("gate_norm", l, t + 1))
                    chain.link(l, G.tensor_tensor(zv[:, t, :], zv[:, t, :], ln_rows[:, 0, :], ALU.mult))
                    signal(G.tensor_tensor(zv[:, t, :], zv[:, t, :], ln_rows[:, 1, :], ALU.add), "gate_v")
                rope(l, ibuf, tmp_b, IDX_HEADS + 1, 32, "sin_i", 0, [U["I0"], U["I1"], U["I2"]])
                for t in range(NT):
                    pool.wait_ge(*at("score_done", l, t + 1))
                    w = work[:, t, 0:(t + 1) * P]
                    signal(G.affine_select(out=w, in_=w, compare_op=ALU.is_ge, fill=NEG, base=t * P,
                                           pattern=[[-1, (t + 1) * P]], channel_multiplier=1), "masked")
                rope(l, cbuf, rope_b, SA_HEADS + 1, 64, "sin_h", 2, [U["C0"], U["C1"]])
                pool.wait_ge(*at("topk_done", l, 1))
                m = mbias[:, 0, 0:P]
                signal(G.affine_select(out=m, in_=m, compare_op=ALU.is_ge, fill=-OFF, base=0, pattern=[[-1, P]],
                                       channel_multiplier=1), "mask_ready")
                triangle_rows(l, 0)
                off_diagonals(l, 0)
                triangle_rows(l, 1)
                off_diagonals(l, 1)
                for n in range(16):
                    q, j = n // 4, n % 4
                    wait_pair_freed(pool, l, U[f"U{q}{j}"])
                    if n >= 2:
                        wait_full(pool, l, ("hT", (n - 2) // 4, (n - 2) % 4, 1))
                    signal(G.tensor_tensor(h_sq[:, j % 2, :], h_relu[:, j % 2, :], h_relu[:, j % 2, :], ALU.mult),
                           "h_sq_ready")

        for name, n in counts.items():
            unit = 16 if name.endswith("landed") else 1
            if unit == 1:
                extra = 8 if name == "ssq_ready" else 0
                assert n == PER_LAYER[name] * DEPTH + extra, (name, n)


_INS = ["x", "mem", "ln_mix", "w_in", "conv_w", "a_log", "dt_bias", "gdn_norm", "sg_ln_g", "sg_ln_b", "sg_w", "sg_b",
        "w_out", "ln_cross", "ln_mem", "w_q_mem", "w_kv_mem", "w_o_mem", "ln_mlp", "w_up", "w_down", "ln_final"]


def kernel(**inputs):
    import concourse.bacc as bacc
    from concourse.bass_utils import run_bass_kernel_spmd

    nc = bacc.Bacc("TRN2", target_bir_lowering=False, num_devices=1)
    arrays = {"consts": shape_constants()}
    args = [nc.dram_tensor("consts", (P, N_CONST), F32, kind="ExternalInput").ap()]
    for name in _INS:
        a = np.ascontiguousarray(inputs[name])
        arrays[name + "_dram"] = a
        args.append(nc.dram_tensor(name + "_dram", a.shape, mybir.dt.from_np(a.dtype), kind="ExternalInput").ap())
    args.append(nc.dram_tensor("out_dram", (1, SEQ, D_MODEL), F32, kind="ExternalOutput").ap())
    trunk(nc, *args)
    r = run_bass_kernel_spmd(nc, [arrays], core_ids=[0])
    return r.results[0]["out_dram"]
```
